# Optimizing a Trainium2 kernel written in Bass

```python
import math, functools
import jax, jax.numpy as jnp
from jax import lax
import numpy as np

D_MODEL = 2048
BATCH = 1
SEQ = 256
DEPTH = 1
DEC_BATCH = 8
DEC_SEQ = 4
PAST_LEN = 256
PAGE_SIZE = 128

MIX_WIDTH = D_MODEL
A_WIDTH = MIX_WIDTH // 2
HEAD_DIM = 128
A_HEADS = A_WIDTH // HEAD_DIM
A_KV_HEADS = 2
IDX_HEADS = 16
IDX_DIM = 64
TOPK_MAX = 256
ATT_BLOCK = 128
NUM_BUCKETS = 32
MAX_DISTANCE = 128
B_WIDTH = MIX_WIDTH // 4
B_HEADS = 4
B_DV = B_WIDTH // B_HEADS
B_DK = B_DV // 2
GATE_RANK = 16
GATE_TEMP = 16.0
GLA_CHUNK = 64
C_WIDTH = MIX_WIDTH - A_WIDTH - B_WIDTH
C_GROUPS = 4
C_GROUP_DIM = C_WIDTH // C_GROUPS
GMLP_CHUNK = 128
FF_DIM = ((8 * D_MODEL // 3 + 255) // 256) * 256
PLE_DIM = 256
EPS = 1e-6

PROJ_SIZES = (A_HEADS * HEAD_DIM, A_KV_HEADS * HEAD_DIM, A_KV_HEADS * HEAD_DIM,
              IDX_HEADS * IDX_DIM, IDX_DIM, IDX_HEADS,
              B_HEADS * B_DK, B_HEADS * B_DK, B_WIDTH, GATE_RANK, B_WIDTH,
              C_WIDTH, C_WIDTH)
PROJ_TOTAL = sum(PROJ_SIZES)

kernel_name = "hybrid_dsa_gla_gmlp_decode_step"

def rmsnorm(x, g):
    xf = x.astype(jnp.float32)
    y = xf * lax.rsqrt(jnp.mean(xf * xf, axis=-1, keepdims=True) + EPS)
    return (y * g.astype(jnp.float32)).astype(x.dtype)

def split_proj(proj):
    out, start = [], 0
    for size in PROJ_SIZES:
        out.append(proj[..., start:start + size])
        start += size
    return out

def rel_bucket(dist):
    n = jnp.maximum(dist, 0)
    max_exact = NUM_BUCKETS // 2
    large = max_exact + (jnp.log(jnp.maximum(n, 1).astype(jnp.float32) / max_exact)
                         / math.log(MAX_DISTANCE / max_exact)
                         * (NUM_BUCKETS - max_exact)).astype(jnp.int32)
    large = jnp.minimum(large, NUM_BUCKETS - 1)
    return jnp.where(n < max_exact, n, large)

def indexer_scores(qi, wi, ki_all):
    s = jnp.einsum('bthd,bld->bthl', qi.astype(jnp.float32), ki_all.astype(jnp.float32)) * IDX_DIM ** -0.5
    return jnp.einsum('bth,bthl->btl', wi.astype(jnp.float32) * IDX_HEADS ** -0.5, jax.nn.relu(s))

def select_keys(scores, t_pos, n_keys, k_sel):
    key_pos = jnp.arange(n_keys)
    admissible = key_pos[None, None, :] <= t_pos[None, :, None]
    scores = jnp.where(admissible, scores, -jnp.inf)
    _, idx = lax.top_k(scores, k_sel)
    valid = idx <= t_pos[None, :, None]
    return idx, valid

def attend_selected(q, k_sel, v_sel, t_pos, sel_pos, valid, rel_bias):
    B_, T_, H_, Dh = q.shape
    G = A_KV_HEADS
    R = H_ // G
    K_ = sel_pos.shape[-1]
    qg = q.reshape(B_, T_, G, R, Dh).astype(jnp.float32)
    logits = jnp.einsum('btgrd,btkgd->btgrk', qg, k_sel.astype(jnp.float32)) * Dh ** -0.5
    bias = rel_bias.astype(jnp.float32)[rel_bucket(t_pos[None, :, None] - sel_pos)]
    bias = bias.reshape(B_, T_, K_, G, R).transpose(0, 1, 3, 4, 2)
    logits = jnp.where(valid[:, :, None, None, :], logits + bias, -1e30)
    p = jax.nn.softmax(logits, axis=-1)
    o = jnp.einsum('btgrk,btkgd->btgrd', p, v_sel.astype(jnp.float32))
    return o.reshape(B_, T_, H_ * Dh).astype(q.dtype)

def _gather_rows(arr, ix):
    return jax.vmap(lambda a, i: a[i])(arr, ix)

def dsa_prompt(q, k, v, qi, wi, ki, rel_bias):
    B_, S_ = q.shape[0], q.shape[1]
    k_sel = min(TOPK_MAX, S_ // 4)
    nb = S_ // ATT_BLOCK

    def to_blocks(x):
        return jnp.moveaxis(x.reshape(B_, nb, ATT_BLOCK, *x.shape[2:]), 1, 0)

    def block(args):
        qb, qib, wib, tb = args
        sc = indexer_scores(qib, wib, ki)
        idx, valid = select_keys(sc, tb, S_, k_sel)
        return attend_selected(qb, _gather_rows(k, idx), _gather_rows(v, idx), tb, idx, valid, rel_bias)

    t_blocks = jnp.arange(S_).reshape(nb, ATT_BLOCK)
    out = lax.map(block, (to_blocks(q), to_blocks(qi), to_blocks(wi), t_blocks))
    return jnp.moveaxis(out, 0, 1).reshape(B_, S_, A_WIDTH)

def dsa_sample(q, k_new, v_new, qi, wi, ki_new, cache_k_l, cache_v_l, cache_ik_l, page_table, rel_bias):
    DB, T_ = q.shape[0], q.shape[1]
    n_pages = page_table.shape[1]
    past = n_pages * PAGE_SIZE
    n_keys = past + T_
    k_sel = min(TOPK_MAX, n_keys // 4)
    t_pos = past + jnp.arange(T_)
    ki_past = cache_ik_l[page_table].reshape(DB, past, IDX_DIM)
    ki_all = jnp.concatenate([ki_past, ki_new.astype(ki_past.dtype)], axis=1)
    sc = indexer_scores(qi, wi, ki_all)
    idx, valid = select_keys(sc, t_pos, n_keys, k_sel)
    in_past = idx < past
    pidx = jnp.minimum(idx, past - 1)
    phys = jnp.take_along_axis(page_table, (pidx // PAGE_SIZE).reshape(DB, -1), axis=1).reshape(idx.shape)
    off = pidx % PAGE_SIZE
    nidx = jnp.clip(idx - past, 0, T_ - 1)

    def sel(cache_l, new):
        return jnp.where(in_past[..., None, None], cache_l[phys, off],
                         _gather_rows(new, nidx).astype(cache_l.dtype))

    return attend_selected(q, sel(cache_k_l, k_new), sel(cache_v_l, v_new), t_pos, idx, valid, rel_bias)

def gla(q, k, v, log_a, s0):
    B_, S_, H_, Dk = q.shape
    Dv = v.shape[-1]
    C = math.gcd(S_, GLA_CHUNK)
    n = S_ // C

    def chunks(x):
        return jnp.moveaxis(x.astype(jnp.float32).reshape(B_, n, C, *x.shape[2:]), 1, 0)

    tri = jnp.tril(jnp.ones((C, C), dtype=bool))

    def step(state, xs):
        qc, kc, vc, gc = xs
        b = jnp.cumsum(gc, axis=1)
        inter = jnp.einsum('bthk,bhkv->bthv', qc * jnp.exp(b), state)
        diff = jnp.where(tri[None, :, :, None, None], b[:, :, None] - b[:, None, :], -jnp.inf)
        att = jnp.einsum('bthk,bshk,btshk->bhts', qc, kc, jnp.exp(diff))
        intra = jnp.einsum('bhts,bshv->bthv', att, vc)
        b_last = b[:, -1]
        new_state = state * jnp.exp(b_last)[..., None] + jnp.einsum(
            'bshk,bshv->bhkv', kc * jnp.exp(b_last[:, None] - b), vc)
        return new_state, inter + intra

    s_fin, o = lax.scan(step, s0.astype(jnp.float32),
                        (chunks(q * B_DK ** -0.5), chunks(k), chunks(v), chunks(log_a)))
    o = jnp.moveaxis(o, 0, 1).reshape(B_, S_, H_, Dv)
    return o, s_fin

def chunk_mlp(uc, vc, g_v, w_spatial, b_spatial):
    B_, S_ = uc.shape[0], uc.shape[1]
    u = jax.nn.gelu(uc)
    vn = rmsnorm(jax.nn.gelu(vc).reshape(B_, S_, C_GROUPS, C_GROUP_DIM), g_v.reshape(C_GROUPS, C_GROUP_DIM))
    pad = (-S_) % GMLP_CHUNK
    n = (S_ + pad) // GMLP_CHUNK
    vp = jnp.pad(vn, ((0, 0), (0, pad), (0, 0), (0, 0))).reshape(B_, n, GMLP_CHUNK, C_GROUPS, C_GROUP_DIM)
    w = w_spatial * jnp.tril(jnp.ones((GMLP_CHUNK, GMLP_CHUNK), w_spatial.dtype))[None]
    s = jnp.einsum('gtj,bnjgc->bntgc', w, vp) + b_spatial.T[None, None, :, :, None]
    s = s.reshape(B_, S_ + pad, C_GROUPS, C_GROUP_DIM)[:, :S_].reshape(B_, S_, C_WIDTH)
    return (u * s).astype(uc.dtype), vn.reshape(B_, S_, C_WIDTH)

def layer_forward(h, p_l, lw, gla_s0, attn_fn):
    B_, S_ = h.shape[0], h.shape[1]
    n = rmsnorm(h, lw['g_mix'])
    q, k, v, qi, ki, wi, qb, kb, vb, gb, rb, uc, vc = split_proj(n @ lw['w_in'])
    q = rmsnorm(q.reshape(B_, S_, A_HEADS, HEAD_DIM), lw['q_norm_g'])
    k = rmsnorm(k.reshape(B_, S_, A_KV_HEADS, HEAD_DIM), lw['k_norm_g'])
    v = v.reshape(B_, S_, A_KV_HEADS, HEAD_DIM)
    qi = qi.reshape(B_, S_, IDX_HEADS, IDX_DIM)
    o_a = attn_fn(q, k, v, qi, wi, ki)
    log_a = jax.nn.log_sigmoid((gb @ lw['w_gate_b'] + lw['b_gate_b']).astype(jnp.float32)) / GATE_TEMP
    o_b, s_b = gla(qb.reshape(B_, S_, B_HEADS, B_DK), kb.reshape(B_, S_, B_HEADS, B_DK),
                   vb.reshape(B_, S_, B_HEADS, B_DV), log_a.reshape(B_, S_, B_HEADS, B_DK), gla_s0)
    o_b = rmsnorm(o_b, lw['g_out_b']).reshape(B_, S_, B_WIDTH).astype(h.dtype) * jax.nn.silu(rb)
    o_c, v_rows = chunk_mlp(uc, vc, lw['g_v_c'], lw['w_spatial'], lw['b_spatial'])
    h = h + jnp.concatenate([o_a, o_b, o_c], axis=-1) @ lw['w_out']
    n2 = rmsnorm(h, lw['g_ffn'])
    h = h + (jax.nn.silu(n2 @ lw['w_ffn_gate']) * (n2 @ lw['w_ffn_up'])) @ lw['w_ffn_down']
    gate = jax.nn.sigmoid(rmsnorm(h, lw['g_ple']) @ lw['w_ple_gate'])
    h = h + gate * (p_l @ lw['w_ple_proj'])
    return h, (k, v, ki, s_b, v_rows)

def setup_inputs(seed: int = 0) -> dict:
    key = jax.random.key(seed)
    ks = jax.random.split(key, 32)
    f32 = jnp.float32

    def nrm(k, shape, scale=1.0):
        return jax.random.normal(k, shape, f32) * scale

    def gain(k, shape):
        return 1.0 + 0.1 * jax.random.normal(k, shape, f32)

    n_pages = PAST_LEN // PAGE_SIZE
    in_use = DEC_BATCH * n_pages
    n_pool = in_use + max(1, in_use // 4)
    page_table = jax.random.permutation(ks[0], n_pool)[:in_use].reshape(DEC_BATCH, n_pages).astype(jnp.int32)
    return {
        'x_prompt': nrm(ks[1], (BATCH, SEQ, D_MODEL)),
        'x_sample': nrm(ks[2], (DEC_BATCH, DEC_SEQ, D_MODEL)),
        'cache_k': nrm(ks[3], (DEPTH, n_pool, PAGE_SIZE, A_KV_HEADS, HEAD_DIM)),
        'cache_v': nrm(ks[4], (DEPTH, n_pool, PAGE_SIZE, A_KV_HEADS, HEAD_DIM)),
        'cache_idx_k': nrm(ks[5], (DEPTH, n_pool, PAGE_SIZE, IDX_DIM)),
        'state_gla': nrm(ks[6], (DEPTH, DEC_BATCH, B_HEADS, B_DK, B_DV), 0.5),
        'page_table': page_table,
        'p_prompt': nrm(ks[7], (DEPTH, BATCH, SEQ, PLE_DIM)),
        'p_sample': nrm(ks[8], (DEPTH, DEC_BATCH, DEC_SEQ, PLE_DIM)),
        'g_mix': gain(ks[9], (DEPTH, D_MODEL)),
        'w_in': nrm(ks[10], (DEPTH, D_MODEL, PROJ_TOTAL), D_MODEL ** -0.5),
        'q_norm_g': gain(ks[11], (DEPTH, HEAD_DIM)),
        'k_norm_g': gain(ks[12], (DEPTH, HEAD_DIM)),
        'rel_bias': nrm(ks[13], (NUM_BUCKETS, A_HEADS), 0.5),
        'w_gate_b': nrm(ks[14], (DEPTH, GATE_RANK, B_HEADS * B_DK), GATE_RANK ** -0.5),
        'b_gate_b': nrm(ks[15], (DEPTH, B_HEADS * B_DK), 0.1),
        'g_out_b': gain(ks[16], (DEPTH, B_DV)),
        'g_v_c': gain(ks[17], (DEPTH, C_WIDTH)),
        'w_spatial': nrm(ks[18], (DEPTH, C_GROUPS, GMLP_CHUNK, GMLP_CHUNK), GMLP_CHUNK ** -0.5),
        'b_spatial': gain(ks[19], (DEPTH, C_GROUPS, GMLP_CHUNK)),
        'w_out': nrm(ks[20], (DEPTH, MIX_WIDTH, D_MODEL), MIX_WIDTH ** -0.5),
        'g_ffn': gain(ks[21], (DEPTH, D_MODEL)),
        'w_ffn_gate': nrm(ks[22], (DEPTH, D_MODEL, FF_DIM), D_MODEL ** -0.5),
        'w_ffn_up': nrm(ks[23], (DEPTH, D_MODEL, FF_DIM), D_MODEL ** -0.5),
        'w_ffn_down': nrm(ks[24], (DEPTH, FF_DIM, D_MODEL), FF_DIM ** -0.5),
        'g_ple': gain(ks[25], (DEPTH, D_MODEL)),
        'w_ple_gate': nrm(ks[26], (DEPTH, D_MODEL, D_MODEL), D_MODEL ** -0.5),
        'w_ple_proj': nrm(ks[27], (DEPTH, PLE_DIM, D_MODEL), PLE_DIM ** -0.5),
    }

def reference(x_prompt, x_sample, cache_k, cache_v, cache_idx_k, state_gla, page_table,
              p_prompt, p_sample, g_mix, w_in, q_norm_g, k_norm_g, rel_bias, w_gate_b, b_gate_b,
              g_out_b, g_v_c, w_spatial, b_spatial, w_out, g_ffn, w_ffn_gate, w_ffn_up, w_ffn_down,
              g_ple, w_ple_gate, w_ple_proj):
    hp, hs = x_prompt, x_sample
    n_batch = x_prompt.shape[0]
    kp, vp, ikp, sp = [], [], [], []
    ksm, vsm, iks, ss, cs = [], [], [], [], []
    attn_prompt = functools.partial(dsa_prompt, rel_bias=rel_bias)
    for i in range(DEPTH):
        lw = dict(g_mix=g_mix[i], w_in=w_in[i], q_norm_g=q_norm_g[i], k_norm_g=k_norm_g[i],
                  w_gate_b=w_gate_b[i], b_gate_b=b_gate_b[i], g_out_b=g_out_b[i], g_v_c=g_v_c[i],
                  w_spatial=w_spatial[i], b_spatial=b_spatial[i], w_out=w_out[i], g_ffn=g_ffn[i],
                  w_ffn_gate=w_ffn_gate[i], w_ffn_up=w_ffn_up[i], w_ffn_down=w_ffn_down[i],
                  g_ple=g_ple[i], w_ple_gate=w_ple_gate[i], w_ple_proj=w_ple_proj[i])
        s0 = jnp.zeros((n_batch, B_HEADS, B_DK, B_DV), jnp.float32)
        hp, (k_p, v_p, ik_p, s_p, _) = layer_forward(hp, p_prompt[i], lw, s0, attn_prompt)
        kp.append(k_p); vp.append(v_p); ikp.append(ik_p); sp.append(s_p)
        attn_sample = functools.partial(dsa_sample, cache_k_l=cache_k[i], cache_v_l=cache_v[i],
                                        cache_ik_l=cache_idx_k[i], page_table=page_table, rel_bias=rel_bias)
        hs, (k_s, v_s, ik_s, s_s, c_s) = layer_forward(hs, p_sample[i], lw, state_gla[i], attn_sample)
        ksm.append(k_s); vsm.append(v_s); iks.append(ik_s); ss.append(s_s); cs.append(c_s)
    return (hp, hs, jnp.stack(kp), jnp.stack(vp), jnp.stack(ikp), jnp.stack(sp),
            jnp.stack(ksm), jnp.stack(vsm), jnp.stack(iks), jnp.stack(ss), jnp.stack(cs))


_drawn_inputs = setup_inputs


def setup_inputs(seed=0):
    import zlib

    import numpy as np

    out = dict(_drawn_inputs(seed))
    spreads = {}
    factors = {'q_norm_g': 3.61, 'g_ple': 3.611}
    for name, (base, spread) in spreads.items():
        noise = np.random.default_rng([zlib.crc32(name.encode()), seed]).standard_normal(out[name].shape)
        drawn = base * np.exp(spread * noise) if base else spread * noise
        out[name] = __import__('jax').numpy.asarray(drawn.astype(out[name].dtype))
    for name, factor in factors.items():
        out[name] = (out[name] * factor).astype(out[name].dtype)
    return out
```

```python
from contextlib import ExitStack, contextmanager

import numpy as np

import concourse.bass as bass
from concourse import mybir

F32 = mybir.dt.float32
F32R = mybir.dt.float32r
I32 = mybir.dt.int32
U32 = mybir.dt.uint32
ALU = mybir.AluOpType
ACT = mybir.ActivationFunctionType
AX = mybir.AxisListType

P = 128
D = 2048
KT = D // P
SEQ, NB, NS = 256, 8, 4
TS = NB * NS
T = SEQ + TS
HD, NH, NG = 128, 8, 2
NR = NH // NG
IH, ID = 16, 64
PAST, PAGE, NPOOL = 256, 128, 20
NPG = PAST // PAGE
KSEL_P, KSEL_S = 64, 65
BH, BDK, BDV, RANK = 4, 64, 128, 16
FF, PLE = 5632, 256
EPS = 1e-6
GATE_TEMP = 16.0
NBUCKET, MAXDIST = 32, 128

ROW_Q, ROW_RB, ROW_UC, ROW_K, ROW_V, ROW_QI, ROW_KI, ROW_MISC = 0, 8, 12, 16, 18, 20, 28, 29
ROW_QB, ROW_KB, ROW_VB, ROW_VC = 30, 32, 34, 38
N_IN = 42
FIRST_ROWS = 10
ORDER = (*range(ROW_QI, ROW_QI + FIRST_ROWS), *range(ROW_Q, ROW_Q + 8), *range(ROW_K, ROW_K + 4),
         *range(ROW_QB, ROW_QB + 12), *range(ROW_RB, ROW_RB + 4), *range(ROW_UC, ROW_UC + 4))
GB0 = 32
N_OUT = D // P
FT = FF // P
HALVES = 2
FH = FT // HALVES
DK = FH // 2
GK = KT + PLE // P

NEG, MARK, TOP, BIG = -3.0e38, float(np.float32(-3.39e38)), 3.0e38, 1.0e30
DMAX = PAST + NS - 1
NDIST = 388
LEVELS = [64, 32, 16, 8, 4, 2, 1]
NORMS = [(ROW_Q, 0), (ROW_Q + 2, 0), (ROW_Q + 4, 0), (ROW_Q + 6, 0), (ROW_K, 1), (ROW_VC, 5), (ROW_VC + 2, 7)]

TIMETABLE = {
    10: [("weights", 0), ("bias_in", 0)],
    11: [("index", 0), ("index_s", 0), ("index", 1), ("index_s", 1)],
    12: [("index", 2), ("index_s", 2), ("index", 3), ("index_s", 3)],
    13: [("index", 4), ("index_s", 4), ("index", 5), ("index_s", 5)],
    14: [("index", 6), ("index_s", 6), ("index", 7), ("index_s", 7)],
    15: [("index_end", 0), ("pick", (0, 0, 4))],
    16: [("norm", 0), ("pick", (0, 4, 8))],
    17: [("norm", 1), ("pick", (1, 0, 3))],
    18: [("pick", (1, 3, 6))],
    19: [("norm", 2), ("pick", (1, 6, 8))],
    20: [("norm", 3), ("pick_s", (0, 3))],
    21: [("norm", 4), ("pick_s", (3, 6))],
    22: [("values", 0), ("pick_s", (6, 9))],
    23: [("softmax", 0)],
    24: [("transpose", 0)],
    25: [("mix", 0), ("softmax", 1)],
    26: [("gate", 0), ("transpose", 1)],
    27: [("mix", 1), ("scan", 0)],
    28: [("softmax", 2), ("level", 0)],
    29: [("transpose", 2), ("level", 1)],
    30: [("mix", 2), ("level", 2)],
    31: [("softmax", 3), ("level", 3)],
    32: [("transpose", 3), ("level", 4)],
    33: [("mix", 3), ("level", 5)],
    34: [("level", 6)],
    35: [("gelu_v", 0), ("level", 7)],
    36: [("level", 8)],
    37: [("level_s", 0), ("last", 0)],
    38: [("norm", 5)],
    39: [("norm", 6), ("decayed", 0)],
    40: [("vn_nat", 0)],
    41: [("keys_s", 0), ("gate_rows", 0)],
}
AFTER = [("vb_nat", 0), ("softmax_s", 0), ("kd_nat", 0), ("state_s_mask", 0), ("transpose_s", 0), ("outputs", 0),
         ("mix_s", 0), ("state_p", 0), ("softmax_s", 1), ("out_norm", 0), ("transpose_s", 1), ("state_s", 0),
         ("mix_s", 1), ("spatial", 0)]

CONST = {"ident": (P, P), "bigI": (P, P), "lev": (P, 7 * P), "tril": (P, P), "wsm": (TS, TS),
         "scan": (P, T), "e16": (IH, 64), "wbm": (64, NB * TS), "adm": (TS, TS), "admneg": (TS, TS),
         "ex": (TS, 2 * P), "eb": (TS, P), "blk": (TS, NB), "bucket": (NBUCKET, NDIST)}


def const_columns():
    at, out = 0, {}
    for name, (rows, cols) in CONST.items():
        out[name] = (rows, at, cols)
        at += cols
    return out, at


def constants():
    where, total = const_columns()
    c = np.zeros((P, total), np.float32)

    def put(name, a):
        rows, at, cols = where[name]
        c[:rows, at:at + cols] = np.asarray(a, np.float32).reshape(rows, cols)

    p = np.arange(P)
    put("ident", np.eye(P))
    put("bigI", np.eye(P) * BIG)
    s, t = p[:, None], p[None, :]
    put("lev", np.stack([(s // (2 * L) == t // (2 * L)) & (s % (2 * L) < L) & (t % (2 * L) >= L)
                         for L in LEVELS], 1))
    put("tril", s <= t)
    b, i = np.arange(TS) // NS, np.arange(TS) % NS
    same = b[:, None] == b[None, :]
    put("wsm", same & (i[:, None] <= i[None, :]))
    scan = np.ones((P, T))
    scan[:, 0] = 0
    scan[:, SEQ::NS] = 0
    put("scan", scan)
    e, j, tq = np.arange(64) // 32, np.arange(64) % 32 // NS, np.arange(64) % NS
    put("e16", np.arange(IH)[:, None] == (2 * j + e)[None, :])
    put("wbm", ((b[None, None, :] == np.arange(NB)[None, :, None]) & (i[None, None, :] == tq[:, None, None]))
        * (ID ** -0.5 * IH ** -0.5))
    adm = same & (i[None, :] <= i[:, None])
    put("adm", adm)
    put("admneg", np.where(adm, 0.0, NEG))
    rb, rt, rh = np.arange(P) // 32, np.arange(P) % 32 // NH, np.arange(P) % NH
    put("ex", np.stack([(b[:, None] == (4 * x + rb)[None, :]) & (i[:, None] == rt[None, :])
                        for x in range(2)], 1) * BIG)
    put("eb", np.arange(32)[:, None] == (rt * NH + rh)[None, :])
    put("blk", b[:, None] == np.arange(NB)[None, :])
    dist = np.maximum(DMAX - np.arange(NDIST), 0)
    half = NBUCKET // 2
    large = half + (np.log(np.maximum(dist, 1).astype(np.float32) / half)
                    / np.float32(np.log(MAXDIST / half)) * (NBUCKET - half)).astype(np.int32)
    bucket = np.where(dist < half, dist, np.minimum(large, NBUCKET - 1))
    put("bucket", np.arange(NBUCKET)[:, None] == bucket[None, :])
    return c


class Steps:

    def __init__(self, eng, sem):
        self.eng, self.sem, self.n = eng, sem, 0

    def __call__(self, ins):
        self.n += 1
        ins.then_inc(self.sem, 1)
        self.eng.wait_ge(self.sem, self.n)

    @contextmanager
    def each(self, i, count, per):
        base, k = self.n, [0]

        def link(ins):
            k[0] += 1
            ins.then_inc(self.sem, 1)
            self.eng.wait_ge(self.sem, i * per + (base + k[0]))

        yield link
        assert k[0] == per, (k[0], per)
        self.n = base + per * count


def build_layer(nc, a, o):
    es = ExitStack()
    with es:
        def sb(name, shape, dt=F32, ctx=es):
            return ctx.enter_context(nc.sbuf_tensor(name, shape, dt))

        sems = {}

        def S(name):
            if name not in sems:
                sems[name] = es.enter_context(nc.semaphore(name))
            return sems[name]

        RW = GK * P
        raw = sb("w_raw", [P, 2, RW])
        whi = sb("w_hi", [P, 2, RW], F32R)
        wlo = sb("w_lo", [P, 2, RW], F32R)
        ones = sb("ones", [P, P])
        rstd = sb("rstd", [P, T])
        ssq = sb("ssq", [P, T])
        sqt = sb("sqt", [P, T])
        gains = sb("gains", [P, 3, KT])
        small = sb("small", [P, 16])
        pages = sb("pages", [1, NB * NPG], I32)
        tmp = sb("tmp", [P, 3, T])
        tmp1, tmp2, tmp3 = tmp[:, 0, :], tmp[:, 1, :], tmp[:, 2, :]
        epsc = sb("epsc", [P, 1])

        proj_ctx = ExitStack()
        proj = sb("proj", [P, N_IN, T], ctx=proj_ctx)
        where, n_const = const_columns()
        consts = sb("consts", [P, n_const], ctx=proj_ctx)
        C = {n: consts[0:r, at:at + cols] for n, (r, at, cols) in where.items()}
        bias_p = sb("bias_p", [P, NH, SEQ], ctx=proj_ctx)
        bias_s = sb("bias_s", [TS, T], ctx=proj_ctx)
        bias_n = sb("bias_n", [TS, NS], ctx=proj_ctx)
        vnat = sb("vnat", [P, 3, NG * HD], ctx=proj_ctx)
        wi_n = sb("wi_n", [P, 2, IH], ctx=proj_ctx)
        sc = sb("sc", [P, 2, SEQ], ctx=proj_ctx)
        top8 = sb("top8", [P, 8], ctx=proj_ctx)
        sc_s = sb("sc_s", [TS, T + 7], ctx=proj_ctx)
        top8s = sb("top8s", [TS, 8], ctx=proj_ctx)
        sm = sb("sm", [P, 20], ctx=proj_ctx)
        wgb = sb("wgb", [P, 256], ctx=proj_ctx)
        lg2 = sb("lg2", [P, 4, T], ctx=proj_ctx)
        la, lsp = lg2[:, 0:2, :], lg2[:, 2:4, :]
        bc = sb("bc", [P, 2, T], ctx=proj_ctx)
        dd = sb("dd", [P, 2, 2, T], ctx=proj_ctx)
        ebs = sb("ebs", [P, 2, TS], ctx=proj_ctx)
        qes = sb("qes", [P, 2, TS], ctx=proj_ctx)
        att = sb("att", [P, 2, 4, P], ctx=proj_ctx)
        att_c = sb("att_c", [P, 2, 2, P], ctx=proj_ctx)
        att_s = sb("att_s", [TS, 2, 2 * TS], ctx=proj_ctx)
        ix_ctx = ExitStack()
        rl = sb("rl", [P, 4, SEQ], ctx=ix_ctx)
        ki_s = sb("ki_s", [P, 2, T], ctx=ix_ctx)
        rl_s = sb("rl_s", [64, 2, T], ctx=ix_ctx)
        wb = sb("wb", [64, NB, TS], ctx=ix_ctx)
        qi_s = sb("qi_s", [P, NB, 32], ctx=ix_ctx)
        btab = sb("btab", [NH, NDIST], ctx=ix_ctx)
        relb = sb("relb", [NBUCKET, NH], ctx=ix_ctx)
        ix_ctx.close()
        prob = sb("prob", [P, NR * SEQ], ctx=proj_ctx)
        pt = sb("pt", [P, 2 * NR * P], ctx=proj_ctx)
        qpad = sb("qpad", [P, NB, NG, 32], ctx=proj_ctx)
        sp_o = sb("sp_o", [P, 2, BDV], ctx=proj_ctx)
        spare = sb("spare", [P, 350], ctx=proj_ctx)
        in_ctx = ExitStack()
        x_hi = sb("x_hi", [P, KT, T], F32R, ctx=in_ctx)
        x_lo = sb("x_lo", [P, KT, T], F32R, ctx=in_ctx)
        in_ctx.close()
        la_ctx = ExitStack()
        k_s = sb("k_s", [P, 4, NG, T], ctx=la_ctx)
        v_s = sb("v_s", [P, 4, NPG, NG * HD], ctx=la_ctx)
        s0 = sb("s0", [P, NB, 2, BDV], ctx=la_ctx)
        vbn = sb("vbn", [P, 3, 512], ctx=la_ctx)
        kdn = sb("kdn", [P, 3, 256], ctx=la_ctx)
        la_ctx.close()
        proj_ctx.close()
        x_f = proj[:, 0:KT, :]
        qk = proj[:, ROW_QI:ROW_QI + 8, :].rearrange("p (z n r) t -> p z n r t", z=2, n=2)
        qe, ke = qk[:, 0], qk[:, 1]
        kdm = proj[0:TS, ROW_QI:ROW_QI + 8, :].rearrange("p a t -> p (a t)")[:, 0:NB * 256]\
            .rearrange("p (b n) -> p b n", b=NB)
        prob_s = prob[:, 0:2 * T].rearrange("p (x s) -> p x s", x=2)
        pt_s = pt[:, 0:6 * P].rearrange("p (x s) -> p x s", x=2)
        sqb = tmp[:, 0:2, :]
        kdT = tmp[:, 0:2, :]
        ob = dd[:, :, :, :].rearrange("p a r t -> p (a r) t")
        osq = gsum = proj[:, ROW_VB:ROW_VB + 4, :]
        vnn = bias_p[:, 0:6, :].rearrange("p a b -> p (a b)").rearrange("p (a b) -> p a b", a=3)
        flat = lg2[:, :, :].rearrange("p a t -> p (a t)")
        ws = flat[:, 0:4 * P].rearrange("p (g t) -> p g t", g=4)
        bsp = flat[:, 4 * P:8 * P].rearrange("p (g t) -> p g t", g=4)
        wss = flat[0:TS, 8 * P:8 * P + 4 * TS].rearrange("p (g t) -> p g t", g=4)
        n_hi = sb("n_hi", [P, KT, T], F32R)
        h = sb("h", [P, KT, T])
        m_hi = sb("m_hi", [P, KT, T], F32R)
        m_lo = sb("m_lo", [P, KT, T], F32R)
        n_lo = sb("n_lo", [P, KT, T], F32R)
        a_hi = sb("a_hi", [P, FH, T], F32R)
        a_lo = sb("a_lo", [P, FH, T], F32R)
        p_f = sb("p_f", [P, 2, T])
        p_hi = m_hi[:, 2:4, :]
        p_lo = m_lo[:, 0:2, :]

        acc = es.enter_context(nc.psum_tensor("acc", [P, 2, 512], F32))
        px = es.enter_context(nc.psum_tensor("px", [P, 6, 512], F32))
        table = nc.dram_tensor("bias_table", [NH, P, NDIST], F32, kind="Internal").ap()

        phases = [("in", N_IN, KT, a["w_in"], 0), ("out", N_OUT, KT, a["w_out"], 0)]
        for hf in range(HALVES):
            phases += [(f"up{hf}", 2 * FH, KT, a["w_gu"], hf * 2 * FH),
                       (f"down{hf}", 2 * N_OUT, DK, a["w_down"], hf * 2 * N_OUT)]
        phases += [("ple", N_OUT, GK, a["w_ple"], 0)]
        stream, g0 = {}, 0
        for name, n, kt, src, first in phases:
            stream[name] = (g0, n, kt, src, first)
            g0 += n
        following = {x[0]: y[0] for x, y in zip(phases, phases[1:])}

        def slot_value(G, slot, per):
            return (G - slot) // 2 * per + per if isinstance(G, int) else None

        loaded = [S("w_loaded0"), S("w_loaded1")]

        def load_group(sp, name, i, j):
            base, n, kt, src, first = stream[name]
            G = base + j + i * 2
            if not isinstance(i, int) or G >= 2:
                sp.wait_ge(S("w_lo_done"), G - 1)
            row = src[bass.ds(i * 2 + (first + j), 1), :, :].rearrange("o p n -> (o p) n")
            sp.dma_start(raw[:, j, 0:kt * P], row).then_inc(loaded[j], 16)

        def load_phase(sp, name, done=0):
            base, n, kt, src, first = stream[name]
            for i in range(done // 2, 1 if base == 0 else done // 2):
                for j in range(2):
                    load_group(sp, name, i, j)
            with sp.Fori(max(done // 2, 1 if base == 0 else 0), n // 2) as i:
                for j in range(2):
                    load_group(sp, name, i, j)

        def split_hi(act, name, i, j):
            base, n, kt, src, first = stream[name]
            G = base + j + i * 2
            act.wait_ge(loaded[j], i * 16 + (base // 2 * 16 + 16))
            if not isinstance(i, int) or G >= 2:
                act.wait_ge(S("w_used"), G - 1)
            nc.scalar.activation(whi[:, j, 0:kt * P], raw[:, j, 0:kt * P], ACT.Copy).then_inc(S("w_hi_done"), 1)

        def split_lo(dve, name, i, j):
            base, n, kt, src, first = stream[name]
            G = base + j + i * 2
            dve.wait_ge(S("w_hi_done"), G + 1)
            nc.vector.tensor_tensor(wlo[:, j, 0:kt * P], raw[:, j, 0:kt * P], whi[:, j, 0:kt * P].bitcast(F32),
                                    ALU.subtract).then_inc(S("w_lo_done"), 1)

        def paced(eng, name, split, evict, start=0):
            base, n, *_ = stream[name]
            if n > 2:
                with eng.Fori(start, n // 2 - 1) as i:
                    split(eng, name, i, 1)
                    evict(i, 0)
                    split(eng, name, i + 1, 0)
                    evict(i, 1)
            i = n // 2 - 1
            split(eng, name, i, 1)
            evict(i, 0)
            if name in following:
                split(eng, following[name], 0, 0)
            evict(i, 1)

        def products(out, j, k0, kt, m_hi_, m_lo_, first=True, last=True, at=0):
            for k in range(kt):
                w_h = whi[:, j, (at + k) * P:(at + k + 1) * P]
                w_l = wlo[:, j, (at + k) * P:(at + k + 1) * P]
                nc.tensor.matmul(out, w_h, m_hi_[:, k0 + k, :], start=first and k == 0, stop=False)
                nc.tensor.matmul(out, w_h, m_lo_[:, k0 + k, :], start=False, stop=False)
                ins = nc.tensor.matmul(out, w_l, m_hi_[:, k0 + k, :], start=False, stop=last and k == kt - 1)
            return ins

        block = es.enter_context(nc.Block())

        widths = [P, P, TS]

        tile0, n_tiles = {}, 0
        for name, n, *_ in phases:
            tile0[name] = n_tiles
            n_tiles += n // 2 if name.startswith("down") else n

        def kept(row):
            return ORDER.index(row) + 1

        def do(stages, slot):
            for stage, arg in TIMETABLE.get(slot, ()) if isinstance(slot, int) else slot:
                if stage in stages:
                    stages[stage](arg)

        @block.sync
        def _(sp):
            sp.dma_start(x_f[:, 0:8, :], a["xT"][:, 0:8, :]).then_inc(S("x_loaded"), 16)
            sp.dma_start(gains[:, :, :], a["gains"]).then_inc(S("small_loaded"), 16)
            sp.dma_start(small[:, 0:9], a["small"]).then_inc(S("small_loaded"), 16)
            sp.dma_start(x_f[:, 8:16, :], a["xT"][:, 8:16, :]).then_inc(S("x_loaded2"), 16)
            for j in range(2):
                load_group(sp, "in", 0, j)
            sp.dma_start(consts[:, :], a["consts"]).then_inc(S("consts_loaded"), 16)
            sp.dma_start(relb[:, :], a["rel_bias"]).then_inc(S("consts_loaded"), 16)
            sp.dma_start(wgb[GB0:GB0 + RANK, :], a["w_gate_b"]).then_inc(S("wgb_loaded"), 16)
            load_phase(sp, "in", done=2)
            for j in range(2):
                load_group(sp, "out", 0, j)
            sp.wait_ge(S("norm_done"), 5)
            sp.dma_start(o["kvT"][:, 0:4, :], proj[:, ROW_K:ROW_K + 4, :]).then_inc(S("stored"), 16)
            sp.dma_start(o["kiT"], proj[0:ID, ROW_KI, :]).then_inc(S("stored"), 16)
            sp.wait_ge(S("norm_done"), 7)
            sp.dma_start(o["vn_s"], proj[:, ROW_VC:ROW_VC + 4, SEQ:T]).then_inc(S("stored"), 16)
            sp.wait_ge(S("w_used"), N_IN)
            sp.dma_start(s0[:, :, :, :], a["state"]).then_inc(S("s0_loaded"), 16)
            sp.wait_ge(S("state_p_ready"), 1)
            sp.dma_start(o["gla_p"], sp_o[:, :, :]).then_inc(S("stored"), 16)
            sp.wait_ge(S("state_s_ready"), 1)
            sp.dma_start(o["gla_s"], s0[:, :, :, :]).then_inc(S("stored"), 16)
            sp.wait_ge(S("stored"), 16 * 5)
            sp.wait_ge(S("mix_ready"), 3)
            sp.dma_start(h[:, :, :], a["xT"]).then_inc(S("h_loaded"), 16)
            load_phase(sp, "out", done=2)
            for hf in range(HALVES):
                load_phase(sp, f"up{hf}")
                if hf == 0:
                    sp.dma_start(p_f[:, :, :], a["pT"]).then_inc(S("p_loaded"), 16)
                load_phase(sp, f"down{hf}")
            load_phase(sp, "ple")
            sp.wait_ge(S("y_ready"), KT)
            sp.dma_start(o["yT"], h[:, :, :]).then_inc(S("stored"), 16)
            sp.wait_ge(S("stored"), 16 * 6)

        @block.gpsimd
        def _(pool):
            link = Steps(pool, S("pool_step"))
            nc.gpsimd.memset(epsc[:, :], EPS)
            nc.gpsimd.memset(ones[:, :], 1.0).then_inc(S("ones_ready"), 1)
            nc.gpsimd.memset(att[:, :, :, :], 0.0)
            nc.gpsimd.memset(att_s[:, :, :], 0.0)
            nc.gpsimd.memset(sc_s[:, T:T + 7], TOP).then_inc(S("att_zero"), 1)
            nc.gpsimd.dma_start(pages[:, :], a["pages"]).then_inc(S("pages_loaded"), 16)
            pool.wait_ge(S("pages_loaded"), 16)

            def page(b, n):
                return pool.value_load(pages[0:1, b * NPG + n:b * NPG + n + 1], min_val=0, max_val=NPOOL - 1)

            def index_keys(b):
                if b >= 2:
                    pool.wait_ge(S("idx_s_mm"), b - 1)
                for n in range(NPG):
                    src = a["cache_ik"][bass.ds(page(b, n), 1), :, :].rearrange("o p n -> (o p) n")
                    pool.dma_start(ki_s[:, b % 2, n * PAGE:(n + 1) * PAGE], src).then_inc(S(f"ki_page{b % 2}"), 16)

            diag = [sc[:, 0, 0:P], sc[:, 1, P:SEQ]]

            def mask_scores(tt):
                pool.wait_ge(S("rl_free"), 4 * tt + 4)
                nc.gpsimd.affine_select(out=diag[tt], in_=diag[tt], compare_op=ALU.is_ge, fill=NEG, base=0,
                                        pattern=[[-1, P]], channel_multiplier=1).then_inc(S("scores_masked"), 1)

            def mask_choice(tt):
                pool.wait_ge(S("picked"), tt + 1)
                nc.gpsimd.affine_select(out=diag[tt], in_=diag[tt], compare_op=ALU.is_ge, fill=-1.0, base=0,
                                        pattern=[[-1, P]], channel_multiplier=1).then_inc(S("sel_ready"), 1)

            for b in range(6):
                index_keys(b)
            mask_scores(0)
            index_keys(6)
            index_keys(7)
            mask_scores(1)
            mask_choice(0)
            mask_choice(1)
            pool.wait_ge(S("scanned"), 1)
            pool.dma_start(ws, a["w_sp"]).then_inc(S("gm_loaded"), 16)
            pool.dma_start(wss, a["w_sps"]).then_inc(S("gm_loaded"), 16)
            pool.dma_start(bsp.rearrange("p g t -> p (g t)"), a["b_sp"].partition_broadcast(P)).then_inc(S("gm_loaded"), 16)
            pool.wait_ge(S("gm_loaded"), 48)
            nc.gpsimd.tensor_tensor(ws, ws, C["tril"].unsqueeze(1).broadcast_to([P, 4, P]), ALU.mult)
            nc.gpsimd.tensor_tensor(wss, wss, C["wsm"].unsqueeze(1).broadcast_to([TS, 4, TS]), ALU.mult)\
                .then_inc(S("ws_ready"), 1)
            pool.wait_ge(S("w_used"), N_IN)
            for b in range(NB):
                if b == 4:
                    pool.wait_ge(S("lg_s"), 1)
                for n in range(NPG):
                    pid = page(b, n)
                    pool.dma_start(k_s[:, b % 4, :, n * PAGE:(n + 1) * PAGE],
                                   a["cache_k"][bass.ds(pid, 1), :, :, :].rearrange("o p g n -> (o p) g n"))\
                        .then_inc(S(f"k_page{b % 4}"), 16)
                    if b < 4:
                        pool.dma_start(v_s[:, b % 4, n, :], a["cache_v"][bass.ds(pid, 1), :, :]
                                       .rearrange("o p n -> (o p) n")).then_inc(S(f"v_page{b % 4}"), 16)
            pool.wait_ge(S("pv_s_mm"), 1)
            for b in range(4, NB):
                for n in range(NPG):
                    pool.dma_start(v_s[:, b % 4, n, :], a["cache_v"][bass.ds(page(b, n), 1), :, :]
                                   .rearrange("o p n -> (o p) n")).then_inc(S(f"v_page{b % 4}"), 16)
            for nth, name in enumerate(["out", f"down{HALVES - 1}"]):
                pool.wait_ge(S("ms_mm"), nth + 1)
                link(nc.gpsimd.memset(ssq[:, :], 0.0))
                with pool.Fori(0, KT) as m, link.each(m, KT, 1) as lk:
                    pool.wait_ge(S("acc_read"), m + (tile0[name] + 1))
                    hm = h[:, bass.ds(m, 1), :].rearrange("p o t -> p (o t)")
                    lk(nc.gpsimd.tensor_tensor(sqt[:, :], hm, hm, ALU.mult))
                    nc.gpsimd.tensor_tensor(ssq[:, :], ssq[:, :], sqt[:, :], ALU.add).then_inc(S("ssq_added"), 1)
                    pool.wait_ge(S("ssq_added"), m + (nth * KT + 1))

        @block.scalar
        def _(act):
            link = Steps(act, S("act_step"))
            A = nc.scalar.activation

            def root(n):
                act.wait_ge(S("ms_ready"), n + 1)
                A(rstd[:, :], rstd[:, :], ACT.Sqrt).then_inc(S("root_ready"), 1)

            for c in range(2):
                cs = slice(8 * c, 8 * c + 8)
                act.wait_ge(S("x_loaded" if c == 0 else "x_loaded2"), 16)
                if c:
                    act.wait_ge(S("x_ssq"), 1)
                A(proj[:, 32:40, :], x_f[:, cs, :], ACT.Square).then_inc(S("x_sq"), 1)
                act.wait_ge(S("xg_ready"), c + 1)
                A(x_hi[:, cs, :], proj[:, 16 + 8 * c:24 + 8 * c, :], ACT.Copy).then_inc(S("x_hi_ready"), 1)
            split_hi(act, "in", 0, 0)
            split_hi(act, "in", 0, 1)
            root(0)
            act.wait_ge(S("btab_ready"), 1)
            act.dma_start(table, btab[:, :].unsqueeze(1).broadcast_to([NH, P, NDIST])).then_inc(S("table_written"), 16)
            with act.Fori(1, FIRST_ROWS // 2) as i:
                for j in range(2):
                    split_hi(act, "in", i, j)

            def bias_in(_):
                act.wait_ge(S("table_written"), 16)
                for dst, first, rows, keys in ((bias_p[:, :, :], DMAX - P, P, SEQ), (bias_s[:, 0:PAST], DMAX - PAST, NS, PAST),
                                               (bias_n[:, :], DMAX, NS, NS)):
                    src = bass.AP(tensor=table.tensor, offset=first, ap=[[NDIST - 1, rows], [P * NDIST, NH], [1, keys]])
                    act.dma_start(dst, src).then_inc(S("bias_loaded"), 16)

            def index(st):
                nk = P * (st // 4 + 1)
                act.wait_ge(S("idx_mm"), st + 1)
                if st:
                    act.wait_ge(S("rl_free"), st)
                src = px[:, 0:2, :].rearrange("p e (j s) -> p e j s", j=2)[:, :, :, 0:nk]
                dst = rl[:, :, :].rearrange("p (e j) s -> p e j s", e=2)[:, :, :, 0:nk]
                A(dst, src, ACT.Relu).then_inc(S("relu_done"), 1)

            def index_s(b):
                act.wait_ge(S("idx_s_mm"), b + 1)
                if b >= 2:
                    act.wait_ge(S("idx_s_acc"), b - 1)
                for e in range(2):
                    pp = slice(32 * e, 32 * e + 32)
                    A(rl_s[pp, b % 2, :], px[pp, 4 + e, 0:T], ACT.Relu).then_inc(S("relu_s_done"), 1)

            def norm(n):
                row, _ = NORMS[n]
                if n < 5:
                    act.wait_ge(S("acc_read"), kept(row + 1))
                if n:
                    act.wait_ge(S("norm_done"), n)
                A(sqb, proj[:, row:row + 2, :], ACT.Square).then_inc(S("norm_sq"), 1)
                act.wait_ge(S("norm_mm"), n + 1)
                A(sqb, px[:, 0:2, 0:T], ACT.Sqrt, scale=1.0 / P, bias=epsc[:, 0:1]).then_inc(S("norm_root"), 1)

            def values(_):
                act.wait_ge(S("values_mm"), 1)
                A(vnat[:, 0:2, :].rearrange("p a b -> p (a b)"), px[:, 4, :], ACT.Copy)
                A(vnat[0:TS, 2, :], px[0:TS, 5, 0:256], ACT.Copy).then_inc(S("vnat_ready"), 1)

            def softmax(u):
                nk = P * (u // 2 + 1)
                logits = px[:, 2:4, :].rearrange("p b s -> p (b s)")[:, 0:NR * nk].rearrange("p (r s) -> p r s", r=NR)
                act.wait_ge(S("max_ready"), u + 1)
                if u:
                    act.wait_ge(S("pt_mm"), u)
                for r in range(NR):
                    ins = A(prob[:, r * nk:(r + 1) * nk], logits[:, r, :], ACT.Exp, bias=sm[:, r:r + 1],
                            accum_out=sm[:, 4 + r:5 + r])
                ins.then_inc(S("exp_ready"), 1)

            def transpose(u):
                act.wait_ge(S("pt_mm"), u + 1)
                if u:
                    act.wait_ge(S("mix_mm"), u)
                tiles_ = u // 2 + 1
                A(pt[:, 0:tiles_ * NR * P].rearrange("p (a b) -> p a b", a=tiles_), px[:, 4:4 + tiles_, :], ACT.Copy)\
                    .then_inc(S("pt_ready"), 1)

            def mix(u):
                tt, g = u // 2, u % 2
                act.wait_ge(S("mix_mm"), u + 1)
                A(proj[:, NR * g:NR * g + NR, P * tt:P * tt + P], px[:, 2, :].rearrange("p (r t) -> p r t", r=NR),
                  ACT.Copy).then_inc(S("mix_out"), 1)

            def gate(_):
                act.wait_ge(S("la_ready"), 1)
                link(A(lsp, la, ACT.Abs))
                link(A(lsp, lsp, ACT.Exp, scale=-1.0))
                A(lsp, lsp, ACT.Ln, bias=1.0).then_inc(S("lsp_ready"), 1)

            def decays(n):
                act.wait_ge(S("d_level"), n + 1)
                w = T if n >= 6 else SEQ
                A(dd[:, n % 2, :, 0:w], dd[:, n % 2, :, 0:w], ACT.Exp, scale=1.0 / GATE_TEMP).then_inc(S("e_level"), 1)

            def last(_):
                act.wait_ge(S("d_last"), 1)
                A(dd[:, 1, :, :], dd[:, 1, :, :], ACT.Exp, scale=-1.0 / GATE_TEMP)
                A(ebs[:, :, :], bc[:, :, SEQ:T], ACT.Exp, scale=1.0 / GATE_TEMP).then_inc(S("e_last"), 1)

            def gelu_v(_):
                act.wait_ge(S("acc_read"), kept(ROW_VC + 3))
                link(A(proj[:, ROW_VC:ROW_VC + 4, :], proj[:, ROW_VC:ROW_VC + 4, :], ACT.Gelu_apprx_tanh))

            def gate_rows(_):
                act.wait_ge(S("acc_read"), N_IN)
                A(proj[:, ROW_RB:ROW_RB + 4, :], proj[:, ROW_RB:ROW_RB + 4, :], ACT.Silu).then_inc(S("silu_ready"), 1)
                A(proj[:, ROW_UC:ROW_UC + 4, :], proj[:, ROW_UC:ROW_UC + 4, :], ACT.Gelu_apprx_tanh)\
                    .then_inc(S("gelu_ready"), 1)

            def vn_nat(_):
                act.wait_ge(S("vn_mm"), 1)
                A(vnn[:, 0:2, :], px[:, 4:6, :], ACT.Copy)
                A(vnn[0:TS, 2, :], px[0:TS, 3, :], ACT.Copy).then_inc(S("vnn_ready"), 1)

            def vb_nat(_):
                act.wait_ge(S("vb_mm"), 1)
                A(vbn[:, 0:2, :], px[:, 0:2, :], ACT.Copy)
                A(vbn[0:TS, 2, :], px[0:TS, 4, :], ACT.Copy).then_inc(S("vbn_ready"), 1)

            def kd_nat(_):
                act.wait_ge(S("kd_mm"), 1)
                A(kdn[:, 0:2, :].rearrange("p a b -> p (a b)"), px[:, 5, :], ACT.Copy)
                A(kdn[0:TS, 2, :], px[0:TS, 4, 0:256], ACT.Copy).then_inc(S("kdn_ready"), 1)

            def softmax_s(x):
                act.wait_ge(S("max_s_ready"), x + 1)
                A(prob_s[:, x, :], px[:, 2 + x, 0:T], ACT.Exp, bias=sm[:, 16:17], accum_out=sm[:, 17:18])\
                    .then_inc(S("exp_s_ready"), 1)

            def transpose_s(x):
                act.wait_ge(S("pt_s_mm"), x + 1)
                A(pt_s[:, x, 0:2 * P], px[:, 5, 0:2 * P], ACT.Copy)
                A(pt_s[0:TS, x, 2 * P:3 * P], px[0:TS, 5, 2 * P:3 * P], ACT.Copy).then_inc(S("pt_s_ready"), 1)

            def outputs(_):
                act.wait_ge(S("o_mm"), 1)
                A(ob[:, 0:2, :], acc[:, :, 0:T], ACT.Copy)
                link(A(ob[:, 2:4, :], px[:, 0:2, 0:T], ACT.Copy))
                A(osq, ob[:, :, :], ACT.Square).then_inc(S("osq_ready"), 1)

            def state_p(_):
                act.wait_ge(S("sp_mm"), 1)
                A(sp_o[:, :, :].rearrange("p a b -> p (a b)"), px[:, 4, 0:256], ACT.Copy).then_inc(S("state_p_ready"), 1)

            def out_norm(_):
                act.wait_ge(S("o_ssq"), 1)
                A(osq[:, 0:2, :], acc[:, :, 0:T], ACT.Sqrt, scale=1.0 / BDV, bias=epsc[:, 0:1])
                A(osq[:, 2:4, :], px[:, 0:2, 0:T], ACT.Sqrt, scale=1.0 / BDV, bias=epsc[:, 0:1]).then_inc(S("o_root"), 1)

            def level(m):
                if m + 1 < 8:
                    decays(m + 1)

            stages = dict(bias_in=bias_in, index=index, index_s=index_s, norm=norm, values=values, softmax=softmax,
                          transpose=transpose, mix=mix, gate=gate, scan=lambda _: decays(0), level=level, last=last,
                          gelu_v=gelu_v, gate_rows=gate_rows, vn_nat=vn_nat, vb_nat=vb_nat, kd_nat=kd_nat,
                          softmax_s=softmax_s, transpose_s=transpose_s, outputs=outputs, state_p=state_p,
                          out_norm=out_norm)
            split_hi(act, "in", FIRST_ROWS // 2, 0)
            for t in range(FIRST_ROWS, N_IN):
                if t + 1 < N_IN:
                    split_hi(act, "in", (t + 1) // 2, (t + 1) % 2)
                else:
                    split_hi(act, "out", 0, 0)
                do(stages, t)
            do(stages, AFTER)
            for c in range(4):
                act.wait_ge(S("mix_ready"), 3)
                act.wait_ge(S("stored"), 16 * 5)
                A(m_hi[:, 4 * c:4 * c + 4, :], proj[:, 4 * c:4 * c + 4, :], ACT.Copy).then_inc(S("m_hi_ready"), 1)

            paced(act, "out", split_hi, lambda i, j: None)
            root(1)
            for hf in range(HALVES):
                def gate(i, j):
                    if j == 0:
                        act.wait_ge(S("acc_read"), i * 2 + (tile0[f"up{hf}"] + 1))
                        nc.scalar.activation(tmp2, tmp1, ACT.Silu).then_inc(S("gate_ready"), 1)

                paced(act, f"up{hf}", split_hi, gate)
                paced(act, f"down{hf}", split_hi, lambda i, j: None)
            act.wait_ge(S("p_loaded"), 16)
            nc.scalar.activation(p_hi, p_f[:, :, :], ACT.Copy).then_inc(S("p_hi_ready"), 1)
            root(2)

            def sigmoid(i, j):
                act.wait_ge(S("acc_read"), i * 2 + (tile0["ple"] + j + 1))
                nc.scalar.activation(tmp2, tmp1, ACT.Sigmoid).then_inc(S("ple_gate"), 1)

            paced(act, "ple", split_hi, sigmoid)


        @block.vector
        def _(dve):
            link = Steps(dve, S("dve_step"))
            V = nc.vector

            def inverse_rms(n):
                dve.wait_ge(S("ms_mm"), n + 1)
                V.tensor_scalar(rstd[:, :], px[:, 5, 0:T], 1.0 / D, EPS, ALU.mult, ALU.add).then_inc(S("ms_ready"), 1)
                dve.wait_ge(S("root_ready"), n + 1)
                link(V.reciprocal(rstd[:, :], rstd[:, :]))

            def x_squares(c):
                dve.wait_ge(S("x_sq"), c + 1)
                V.tensor_reduce([ssq[:, :], tmp3][c], proj[:, 32:40, :].rearrange("p k t -> p t k"), AX.X, ALU.add)\
                    .then_inc(S("x_ssq"), 1)

            dve.wait_ge(S("small_loaded"), 32)
            for c in range(2):
                cs, gs = slice(8 * c, 8 * c + 8), slice(16 + 8 * c, 24 + 8 * c)
                dve.wait_ge(S("x_loaded" if c == 0 else "x_loaded2"), 16)
                V.tensor_tensor(proj[:, gs, :], x_f[:, cs, :], gains[:, 0, cs].unsqueeze(2).broadcast_to([P, 8, T]),
                                ALU.mult).then_inc(S("xg_ready"), 1)
                x_squares(c) if c == 0 else None
                dve.wait_ge(S("x_hi_ready"), c + 1)
                V.tensor_tensor(x_lo[:, cs, :], proj[:, gs, :], x_hi[:, cs, :].bitcast(F32), ALU.subtract)\
                    .then_inc(S("x_ready"), 1)
            split_lo(dve, "in", 0, 0)
            x_squares(1)
            dve.wait_ge(S("x_ssq"), 2)
            V.tensor_tensor(ssq[:, :], ssq[:, :], tmp3, ALU.add).then_inc(S("x_ssq"), 1)
            split_lo(dve, "in", 0, 1)
            link(V.tensor_scalar(small[:, 0:1], small[:, 0:1], HD ** -0.5, None, ALU.mult))
            inverse_rms(0)

            def keep(t):
                dve.wait_ge(S("w_used"), t + 1)
                V.tensor_tensor(proj[:, ORDER[t], :], acc[:, t % 2, 0:T], rstd[:, :], ALU.mult).then_inc(S("acc_read"), 1)

            dve.wait_ge(S("btab_mm"), 1)
            V.tensor_copy(btab[:, :], px[0:NH, 3, 0:NDIST]).then_inc(S("btab_ready"), 1)
            keep(0)
            with dve.Fori(1, FIRST_ROWS // 2) as i:
                for j in range(2):
                    split_lo(dve, "in", i, j)
                    dve.wait_ge(S("w_used"), i * 2 + j)
                    V.tensor_tensor(proj[:, bass.ds(i * 2 + (j - 1 + ROW_QI), 1), :].rearrange("p o t -> p (o t)"),
                                    acc[:, 1 - j, 0:T], rstd[:, :], ALU.mult).then_inc(S("acc_read"), 1)
            split_lo(dve, "in", FIRST_ROWS // 2, 0)
            keep(FIRST_ROWS - 1)

            def weights(_):
                dve.wait_ge(S("weights_mm"), 1)
                V.tensor_scalar(wi_n[:, :, :].rearrange("p a b -> p (a b)"), px[:, 3, 0:2 * IH],
                                ID ** -0.5 * IH ** -0.5, None, ALU.mult)
                V.tensor_tensor(wb[:, :, :], px[0:64, 3, 64:64 + TS].unsqueeze(1).broadcast_to([64, NB, TS]),
                                C["wbm"].rearrange("p (b t) -> p b t", b=NB), ALU.mult)
                V.tensor_copy(qi_s[:, :, :].rearrange("p b (j i) -> p b j i", i=NS),
                              proj[:, ROW_QI:ROW_QI + 8, SEQ:T].rearrange("p j (b i) -> p b j i", b=NB))
                V.tensor_copy(ki_s[:, :, PAST:T], proj[:, ROW_KI, SEQ:T].unsqueeze(1).broadcast_to([P, 2, TS]))\
                    .then_inc(S("weights_done"), 1)
                dve.wait_ge(S("weights_done"), 1)

            def index(st):
                tt, q, nk = st // 4, st % 4, P * (st // 4 + 1)
                dve.wait_ge(S("relu_done"), st + 1)
                for e in range(2):
                    for jj in range(2):
                        head = 2 * (2 * q + jj) + e
                        src, w, dst = rl[:, 2 * e + jj, 0:nk], wi_n[:, tt, head:head + 1], sc[:, tt, 0:nk]
                        if q == 0 and e == 0 and jj == 0:
                            ins = V.tensor_scalar(dst, src, w, None, ALU.mult)
                        else:
                            ins = V.scalar_tensor_tensor(dst, src, w, dst, ALU.mult, ALU.add)
                        if (e, jj) != (1, 1):
                            link(ins)
                ins.then_inc(S("rl_free"), 1)
                dve.wait_ge(S("rl_free"), st + 1)

            def index_end(_):
                dve.wait_ge(S("idx_s_acc"), NB)
                V.tensor_copy(sc_s[:, 0:T], px[0:TS, 2, 0:T]).then_inc(S("sc_s_read"), 1)
                dve.wait_ge(S("sc_s_read"), 1)
                link(V.tensor_tensor(sc_s[:, PAST:T], sc_s[:, PAST:T], C["adm"], ALU.mult))
                link(V.tensor_tensor(sc_s[:, PAST:T], sc_s[:, PAST:T], C["admneg"], ALU.add))

            def rounds_of(work, best, rounds):
                for _ in range(rounds):
                    link(V.max(best, work))
                    link(V.match_replace(work, best, work, MARK))

            def pick(arg):
                tt, r0, r1 = arg
                nk = P * (tt + 1)
                if r0 == 0:
                    dve.wait_ge(S("scores_masked"), tt + 1)
                rounds_of(sc[:, tt, 0:nk], top8[:, :], r1 - r0)
                if r1 == KSEL_P // 8:
                    V.tensor_scalar(sc[:, tt, 0:nk], sc[:, tt, 0:nk], MARK, -1.0, ALU.not_equal, ALU.mult)\
                        .then_inc(S("picked"), 1)

            def pick_s(arg):
                r0, r1 = arg
                if r0 == 0:
                    dve.wait_ge(S("att_zero"), 1)
                rounds_of(sc_s[:, :], top8s[:, :], r1 - r0)
                if r1 == (KSEL_S + 7) // 8:
                    V.tensor_scalar(sc_s[:, 0:T], sc_s[:, 0:T], MARK, -1.0, ALU.not_equal, ALU.mult)\
                        .then_inc(S("sel_s_ready"), 1)

            def norm(n):
                row, g = NORMS[n]
                dve.wait_ge(S("norm_root"), n + 1)
                link(V.reciprocal(sqb, sqb))
                if n < 5:
                    rows = proj[:, row:row + 2, :].rearrange("p a t -> p (a t)")
                    ins = V.scalar_tensor_tensor(rows, rows, small[:, g:g + 1], sqb.rearrange("p a t -> p (a t)"),
                                                 ALU.mult, ALU.mult)
                else:
                    for r in range(2):
                        one_ = proj[:, row + r, :]
                        ins = V.scalar_tensor_tensor(one_, one_, small[:, g + r:g + r + 1], sqb[:, r, :],
                                                     ALU.mult, ALU.mult)
                ins.then_inc(S("norm_done"), 1)

            def softmax(u):
                nk = P * (u // 2 + 1)
                logits = px[:, 2:4, :].rearrange("p b s -> p (b s)")[:, 0:NR * nk].rearrange("p (r s) -> p r s", r=NR)
                dve.wait_ge(S("lg_ready"), u + 1)
                V.tensor_reduce(sm[:, 0:4], logits, AX.X, ALU.max, negate=True).then_inc(S("max_ready"), 1)
                dve.wait_ge(S("exp_ready"), u + 1)
                link(V.reciprocal(sm[:, 8:12], sm[:, 4:8]))
                pr = prob[:, 0:NR * nk].rearrange("p (r s) -> p r s", r=NR)
                V.tensor_tensor(pr, pr, sm[:, 8:12].unsqueeze(2).broadcast_to([P, NR, nk]), ALU.mult)\
                    .then_inc(S("p_ready"), 1)

            def gate(_):
                dve.wait_ge(S("gl_gate"), 1)
                for r in range(2):
                    ins = V.tensor_scalar(la[:, r, :], px[:, r, 0:T], small[:, 3 + r:4 + r], None, ALU.add)
                ins.then_inc(S("la_ready"), 1)

            kb, qb = proj[:, ROW_KB:ROW_KB + 2, :], proj[:, ROW_QB:ROW_QB + 2, :]
            levels = [P] + LEVELS

            def by_seq(ap):
                return ap.rearrange("p r (b i) -> p r b i", i=NS)

            def blocks(ap, n):
                L, w = levels[n], (T if levels[n] <= NS // 2 else SEQ)
                v = ap[:, :, 0:w].rearrange("p r (b l) -> p r b l", l=2 * L)
                return v[:, :, :, 0:L], v[:, :, :, L:2 * L], w // (2 * L), L

            def distances(n):
                b1, b2, nb, L = blocks(bc, n)
                d1, d2, _, _ = blocks(dd[:, n % 2, :, :], n)
                mid = b1[:, :, :, L - 1:L].broadcast_to([P, 2, nb, L])
                V.tensor_tensor(d1, mid, b1, ALU.subtract)
                V.tensor_tensor(d2, b2, mid, ALU.subtract).then_inc(S("d_level"), 1)

            def scan(_):
                V.tensor_scalar(qb, qb, BDK ** -0.5, None, ALU.mult).then_inc(S("qb_scaled"), 1)
                dve.wait_ge(S("lsp_ready"), 1)
                flat = [z.rearrange("p a t -> p (a t)") for z in (la, lsp)]
                link(V.scalar_tensor_tensor(flat[0], flat[0], 0.0, flat[1], ALU.min, ALU.subtract))
                for r in range(2):
                    ins = V.tensor_tensor_scan(bc[:, r, :], C["scan"], la[:, r, :], 0.0, ALU.mult, ALU.add)
                ins.then_inc(S("scanned"), 1)
                dve.wait_ge(S("scanned"), 1)
                dve.wait_ge(S("qb_scaled"), 1)
                distances(0)

            def level(m):
                dve.wait_ge(S("level_mm"), m + 1)
                if m == 0:
                    dve.wait_ge(S("att_zero"), 1)
                if m == 1:
                    V.tensor_copy(att_c[:, :, :, :], px[:, 0:2, 0:256].rearrange("p e (r t) -> p e r t", r=2))\
                        .then_inc(S("level_read"), 1)
                else:
                    mask = C["ident"] if m == 0 else C["lev"][:, (m - 2) * P:(m - 1) * P]
                    V.copy_predicated(att[:, :, :, :], mask.bitcast(U32).unsqueeze(1).unsqueeze(1).broadcast_to([P, 2, 4, P]),
                                      px[:, 0:2, :].rearrange("p e (a t) -> p e a t", a=4)).then_inc(S("level_read"), 1)
                    dve.wait_ge(S("level_read"), m + 1)
                if m < 8:
                    dve.wait_ge(S("e_level"), m + 1)
                    e1, e2, _, _ = blocks(dd[:, m % 2, :, :], m)
                    q2, k1 = blocks(qb, m)[1], blocks(kb, m)[0]
                    V.tensor_tensor(blocks(qe[:, m % 2], m)[1], q2, e2, ALU.mult)
                    V.tensor_tensor(blocks(ke[:, m % 2], m)[0], k1, e1, ALU.mult).then_inc(S("level_ready"), 1)
                if m + 1 < 8:
                    distances(m + 1)

            def level_s(_):
                dve.wait_ge(S("level_s_mm"), 1)
                for n in range(3):
                    mask = [C["ident"], C["lev"][:, 5 * P:6 * P], C["lev"][:, 6 * P:7 * P]][n][0:TS, 0:TS].bitcast(U32)
                    ins = V.copy_predicated(att_s[:, :, :].rearrange("p e (r t) -> p e r t", r=2),
                                            mask.unsqueeze(1).unsqueeze(1).broadcast_to([TS, 2, 2, TS]),
                                            px[0:TS, 0:2, 2 * TS * n:2 * TS * (n + 1)].rearrange("p e (r t) -> p e r t", r=2))
                    if n < 2:
                        link(ins)
                ins.then_inc(S("level_s_read"), 1)

            def last(_):
                for r in range(2):
                    V.tensor_scalar(dd[:, 1, r, 0:SEQ], bc[:, r, 0:SEQ], bc[:, r, SEQ - 1:SEQ], None, ALU.subtract)
                bs = by_seq(bc[:, :, SEQ:T])
                V.tensor_tensor(by_seq(dd[:, 1, :, SEQ:T]), bs, bs[:, :, :, NS - 1:NS].broadcast_to([P, 2, NB, NS]),
                                ALU.subtract).then_inc(S("d_last"), 1)

            def decayed(_):
                dve.wait_ge(S("e_last"), 1)
                dve.wait_ge(S("norm_done"), 7)
                V.tensor_tensor(qes[:, :, :], proj[:, ROW_QB:ROW_QB + 2, SEQ:T], ebs[:, :, :], ALU.mult)
                V.tensor_tensor(kdT, kb, dd[:, 1, :, :], ALU.mult).then_inc(S("kd_ready"), 1)

            def keys_s(_):
                link(V.memset(qpad[:, :, :, :], 0.0))
                for g in range(NG):
                    for b in range(NB):
                        V.tensor_copy(qpad[:, b, g, :].rearrange("p (t h) -> p t h", h=NH)[:, :, NR * g:NR * g + NR],
                                      proj[:, NR * g:NR * g + NR, SEQ + NS * b:SEQ + NS * b + NS].rearrange("p r t -> p t r"))
                dve.wait_ge(S("w_used"), N_IN)
                V.tensor_copy(k_s[:, :, :, PAST:T], proj[:, ROW_K:ROW_K + 2, SEQ:T].unsqueeze(1).broadcast_to([P, 4, 2, TS]))
                dve.wait_ge(S("bias_loaded"), 48)
                V.tensor_copy(bias_s[:, PAST:T].rearrange("p (b i) -> p b i", b=NB),
                              bias_n[:, :].unsqueeze(1).broadcast_to([TS, NB, NS])).then_inc(S("keys_s_ready"), 1)

            def softmax_s(x):
                dve.wait_ge(S("lg_s"), x + 1)
                V.tensor_reduce(sm[:, 16:17], px[:, 2 + x, 0:T], AX.X, ALU.max, negate=True).then_inc(S("max_s_ready"), 1)
                dve.wait_ge(S("exp_s_ready"), x + 1)
                link(V.reciprocal(sm[:, 18:19], sm[:, 17:18]))
                V.tensor_scalar(prob_s[:, x, :], prob_s[:, x, :], sm[:, 18:19], None, ALU.mult).then_inc(S("p_s_ready"), 1)

            def mix_s(x):
                dve.wait_ge(S("pv_s_mm"), x + 1)
                for g in range(NG):
                    ins = V.tensor_copy(proj[:, NR * g:NR * g + NR, SEQ + 16 * x:SEQ + 16 * x + 16],
                                        px[:, 2 + x, 64 * g:64 * g + 64].rearrange("p (t r) -> p r t", r=NR))
                if x:
                    ins.then_inc(S("mix_ready"), 1)

            def state_s_mask(_):
                dve.wait_ge(S("kdn_ready"), 1)
                V.tensor_tensor(kdm, kdn[0:TS, 2, :].unsqueeze(1).broadcast_to([TS, NB, 256]),
                                C["blk"].unsqueeze(2).broadcast_to([TS, NB, 256]), ALU.mult).then_inc(S("kdm_ready"), 1)

            def out_norm(_):
                ends = by_seq(ebs[:, :, :])[:, :, :, NS - 1].rearrange("p r b -> p b r")
                dve.wait_ge(S("o_mm"), 1)
                V.tensor_tensor(s0[:, :, :, :], s0[:, :, :, :], ends.unsqueeze(3).broadcast_to([P, NB, 2, BDV]), ALU.mult)\
                    .then_inc(S("s0_decayed"), 1)
                dve.wait_ge(S("o_root"), 1)
                link(V.reciprocal(osq, osq))
                link(V.scalar_tensor_tensor(ob[:, :, :].rearrange("p a t -> p (a t)"), ob[:, :, :].rearrange("p a t -> p (a t)"),
                                            small[:, 2:3], osq.rearrange("p a t -> p (a t)"), ALU.mult, ALU.mult))
                dve.wait_ge(S("silu_ready"), 1)
                V.tensor_tensor(proj[:, ROW_RB:ROW_RB + 4, :], ob[:, :, :], proj[:, ROW_RB:ROW_RB + 4, :], ALU.mult)\
                    .then_inc(S("mix_ready"), 1)

            def state_s(_):
                dve.wait_ge(S("ss_mm"), 1)
                dve.wait_ge(S("s0_decayed"), 1)
                for half, src in ((0, acc), (1, px)):
                    part = s0[:, 4 * half:4 * half + 4, :, :].rearrange("p b r v -> p (b r v)")
                    ins = V.tensor_tensor(part, part, src[:, 0:2, :].rearrange("p a b -> p (a b)"), ALU.add)
                ins.then_inc(S("state_s_ready"), 1)

            def spatial(_):
                dve.wait_ge(S("sp_gm"), 1)
                for half, src in ((0, acc), (1, px)):
                    gs = slice(2 * half, 2 * half + 2)
                    V.tensor_tensor(gsum[:, gs, 0:SEQ].rearrange("p g (c t) -> p g c t", c=2),
                                    src[:, 0:2, 0:SEQ].rearrange("p g (c t) -> p g c t", c=2),
                                    bsp[:, gs, :].unsqueeze(2).broadcast_to([P, 2, 2, P]), ALU.add)
                    ins = V.tensor_tensor(gsum[:, gs, SEQ:T].rearrange("p g (b i) -> p g b i", b=NB),
                                          src[:, 0:2, SEQ:T].rearrange("p g (b i) -> p g b i", b=NB),
                                          bsp[:, gs, 0:NS].unsqueeze(2).broadcast_to([P, 2, NB, NS]), ALU.add)
                ins.then_inc(S("gsum_ready"), 1)
                dve.wait_ge(S("gsum_ready"), 1)
                dve.wait_ge(S("gelu_ready"), 1)
                V.tensor_tensor(proj[:, ROW_UC:ROW_UC + 4, :], gsum, proj[:, ROW_UC:ROW_UC + 4, :], ALU.mult)\
                    .then_inc(S("mix_ready"), 1)

            stages = dict(weights=weights, index=index, index_end=index_end, pick=pick, pick_s=pick_s, norm=norm,
                          softmax=softmax, gate=gate, scan=scan, level=level, level_s=level_s, last=last,
                          decayed=decayed, keys_s=keys_s, softmax_s=softmax_s, mix_s=mix_s, state_s_mask=state_s_mask,
                          out_norm=out_norm, state_s=state_s, spatial=spatial)
            for t in range(FIRST_ROWS, N_IN):
                if t + 1 < N_IN:
                    split_lo(dve, "in", (t + 1) // 2, (t + 1) % 2)
                else:
                    split_lo(dve, "out", 0, 0)
                keep(t)
                do(stages, t)
            do(stages, AFTER)
            dve.wait_ge(S("mix_ready"), 3)
            for c in range(4):
                cs = slice(4 * c, 4 * c + 4)
                dve.wait_ge(S("m_hi_ready"), c + 1)
                V.tensor_tensor(m_lo[:, cs, :], proj[:, cs, :], m_hi[:, cs, :].bitcast(F32), ALU.subtract)\
                    .then_inc(S("m_ready"), 1)

            def one(ap, m):
                return ap[:, bass.ds(m, 1), :].rearrange("p o t -> p (o t)")

            def tile_into_h(m, bank, last_group, tile, gain, lk):
                dve.wait_ge(S("w_used"), last_group)
                hm = one(h, m)
                V.tensor_tensor(hm, hm, acc[:, bank, 0:T], ALU.add).then_inc(S("acc_read"), 1)
                if gain is None:
                    return
                dve.wait_ge(S("acc_read"), tile)
                lk(V.tensor_scalar(tmp1, hm, gains[:, gain, bass.ds(m, 1)], None, ALU.mult))
                lk(V.tensor_copy(one(n_hi, m), tmp1))
                V.tensor_tensor(one(n_lo, m), tmp1, one(n_hi, m).bitcast(F32), ALU.subtract)\
                    .then_inc(S("n_ready"), 1)

            def rounds(name, evict_pair, per):
                base, n, *_ = stream[name]
                if n > 2:
                    with dve.Fori(0, n // 2 - 1) as i, link.each(i, n // 2 - 1, per) as lk:
                        split_lo(dve, name, i, 1)
                        evict_pair(i, 0, lk)
                        split_lo(dve, name, i + 1, 0)
                        evict_pair(i, 1, lk)
                i = n // 2 - 1
                split_lo(dve, name, i, 1)
                evict_pair(i, 0, link)
                if name in following:
                    split_lo(dve, following[name], 0, 0)
                evict_pair(i, 1, link)

            dve.wait_ge(S("h_loaded"), 16)
            b0, t0 = stream["out"][0], tile0["out"]
            rounds("out", lambda i, j, lk: tile_into_h(i * 2 + j, j, i * 2 + (b0 + j + 1), i * 2 + (t0 + j + 1), 1, lk), 4)
            inverse_rms(1)
            for hf in range(HALVES):
                ub, ut = stream[f"up{hf}"][0], tile0[f"up{hf}"]

                def hidden(i, j, lk):
                    dve.wait_ge(S("w_used"), i * 2 + (ub + j + 1))
                    if j == 0:
                        V.tensor_tensor(tmp1, acc[:, 0, 0:T], rstd[:, :], ALU.mult).then_inc(S("acc_read"), 1)
                        return
                    V.tensor_tensor(tmp3, acc[:, 1, 0:T], rstd[:, :], ALU.mult).then_inc(S("acc_read"), 1)
                    dve.wait_ge(S("acc_read"), i * 2 + (ut + 2))
                    dve.wait_ge(S("gate_ready"), i + (hf * FH + 1))
                    lk(V.tensor_tensor(tmp3, tmp3, tmp2, ALU.mult))
                    lk(V.tensor_copy(one(a_hi, i), tmp3))
                    V.tensor_tensor(one(a_lo, i), tmp3, one(a_hi, i).bitcast(F32), ALU.subtract)\
                        .then_inc(S("a_ready"), 1)
                    dve.wait_ge(S("a_ready"), i + (hf * FH + 1))

                rounds(f"up{hf}", hidden, 2)
                db, dt = stream[f"down{hf}"][0], tile0[f"down{hf}"]
                gain = 2 if hf == HALVES - 1 else None
                name = f"down{hf}"
                per = 0 if gain is None else 4
                with dve.Fori(0, N_OUT // 2 - 1) as i, link.each(i, N_OUT // 2 - 1, per) as lk:
                    split_lo(dve, name, i * 2, 1)
                    split_lo(dve, name, i * 2 + 1, 0)
                    tile_into_h(i * 2, 0, i * 4 + (db + 2), i * 2 + (dt + 1), gain, lk)
                    split_lo(dve, name, i * 2 + 1, 1)
                    split_lo(dve, name, i * 2 + 2, 0)
                    tile_into_h(i * 2 + 1, 1, i * 4 + (db + 4), i * 2 + (dt + 2), gain, lk)
                i = N_OUT // 2 - 1
                split_lo(dve, name, i * 2, 1)
                split_lo(dve, name, i * 2 + 1, 0)
                tile_into_h(i * 2, 0, i * 4 + (db + 2), i * 2 + (dt + 1), gain, link)
                split_lo(dve, name, i * 2 + 1, 1)
                split_lo(dve, following[name], 0, 0)
                tile_into_h(i * 2 + 1, 1, i * 4 + (db + 4), i * 2 + (dt + 2), gain, link)
            dve.wait_ge(S("p_hi_ready"), 1)
            V.tensor_tensor(p_lo, p_f[:, :, :], p_hi.bitcast(F32), ALU.subtract).then_inc(S("p_ready2"), 1)
            inverse_rms(2)
            pb, pt0 = stream["ple"][0], tile0["ple"]

            def ple(i, j, lk):
                dve.wait_ge(S("w_used"), i * 2 + (pb + j + 1))
                V.tensor_tensor(tmp1, acc[:, j, 0:T], rstd[:, :], ALU.mult).then_inc(S("acc_read"), 1)
                dve.wait_ge(S("ple_gate"), i * 2 + (j + 1))
                lk(V.tensor_tensor(tmp3, tmp2, px[:, j, 0:T], ALU.mult))
                hm = one(h, i * 2 + j)
                V.tensor_tensor(hm, hm, tmp3, ALU.add).then_inc(S("y_ready"), 1)
                dve.wait_ge(S("y_ready"), i * 2 + (j + 1))

            rounds("ple", ple, 2)


        @block.tensor
        def _(pe):
            M = nc.tensor.matmul
            tr = nc.tensor.transpose
            ident = C["ident"]

            def group(name, i, j, out, k0, kt, hi_, lo_, **kw):
                base = stream[name][0]
                pe.wait_ge(S("w_lo_done"), i * 2 + (base + j + 1))
                products(out, j, k0, kt, hi_, lo_, **kw).then_inc(S("w_used"), 1)

            def tile_free(name, i, per, j):
                if isinstance(i, int) and tile0[name] + per * i + j < 2:
                    return
                pe.wait_ge(S("acc_read"), i * per + (tile0[name] + j - 1))

            def mean_squares(n):
                M(px[:, 5, 0:T], ones[:, :], ssq[:, :], start=True, stop=True).then_inc(S("ms_mm"), 1)

            pe.wait_ge(S("x_ready"), 2)
            pe.wait_ge(S("ones_ready"), 1)
            group("in", 0, 0, acc[:, 0, 0:T], 0, KT, x_hi, x_lo)
            pe.wait_ge(S("x_ssq"), 3)
            mean_squares(0)
            pe.wait_ge(S("consts_loaded"), 32)
            M(px[0:NH, 3, 0:NDIST], relb[:, :], C["bucket"], start=True, stop=True).then_inc(S("btab_mm"), 1)
            group("in", 0, 1, acc[:, 1, 0:T], 0, KT, x_hi, x_lo)
            with pe.Fori(1, FIRST_ROWS // 2) as i:
                for j in range(2):
                    tile_free("in", i, 2, j)
                    group("in", i, j, acc[:, j, 0:T], 0, KT, x_hi, x_lo)

            def weights(_):
                pe.wait_ge(S("acc_read"), kept(ROW_MISC))
                pe.wait_ge(S("btab_ready"), 1)
                for tt in range(2):
                    tr(px[:, 3, IH * tt:IH * tt + IH], proj[0:IH, ROW_MISC, P * tt:P * tt + P], ident[0:IH, 0:IH])
                M(px[0:64, 3, 64:64 + TS], C["e16"], proj[0:IH, ROW_MISC, SEQ:T], start=True, stop=True)\
                    .then_inc(S("weights_mm"), 1)

            def index(st):
                tt, q, nk = st // 4, st % 4, P * (st // 4 + 1)
                if st:
                    pe.wait_ge(S("relu_done"), st)
                for jj in range(2):
                    for e in range(2):
                        pp = slice(64 * e, 64 * e + 64)
                        ins = M(px[:, e, 256 * jj:256 * jj + nk],
                                proj[pp, ROW_QI + 2 * q + jj, P * tt:P * tt + P], proj[pp, ROW_KI, 0:nk],
                                start=True, stop=True)
                ins.then_inc(S("idx_mm"), 1)

            def index_sum(b):
                pe.wait_ge(S("relu_s_done"), 2 * b + 2)
                M(px[0:TS, 2, 0:T], wb[:, b, :], rl_s[:, b % 2, :], start=b == 0, stop=b == NB - 1)\
                    .then_inc(S("idx_s_acc"), 1)

            def index_s(b):
                pe.wait_ge(S("weights_done"), 1)
                pe.wait_ge(S("ms_ready"), 1)
                pe.wait_ge(S(f"ki_page{b % 2}"), 32 * (b // 2 + 1))
                if b:
                    pe.wait_ge(S("relu_s_done"), 2 * b)
                for e in range(2):
                    ins = M(px[32 * e:32 * e + 32, 4 + e, 0:T], qi_s[64 * e:64 * e + 64, b, :],
                            ki_s[64 * e:64 * e + 64, b % 2, :], start=True, stop=True)
                ins.then_inc(S("idx_s_mm"), 1)
                if b:
                    index_sum(b - 1)

            def norm(n):
                if n == 0:
                    pe.wait_ge(S("relu_done"), 8)
                elif n < 5:
                    pe.wait_ge(S("norm_root"), n)
                else:
                    pe.wait_ge(S("norm_root"), n)
                    pe.wait_ge(S("level_s_read"), 1)
                pe.wait_ge(S("norm_sq"), n + 1)
                for r in range(2):
                    ins = M(px[:, r, 0:T], ones[:, :], sqb[:, r, :], start=True, stop=True)
                ins.then_inc(S("norm_mm"), 1)

            def values(_):
                pe.wait_ge(S("relu_s_done"), 2 * NB)
                pe.wait_ge(S("acc_read"), kept(ROW_V + 1))
                for tt, w in enumerate(widths):
                    for g in range(NG):
                        col = 256 * (tt % 2) + g * HD
                        ins = tr(px[0:w, 4 + tt // 2, col:col + HD], proj[:, ROW_V + g, P * tt:P * tt + w], ident)
                ins.then_inc(S("values_mm"), 1)

            def softmax(u):
                tt, g, nk = u // 2, u % 2, P * (u // 2 + 1)
                per = 512 // nk
                if u == 0:
                    pe.wait_ge(S("sc_s_read"), 1)
                    pe.wait_ge(S("bias_loaded"), 48)
                else:
                    pe.wait_ge(S("mix_out"), u)
                pe.wait_ge(S("sel_ready"), tt + 1)
                pe.wait_ge(S("norm_done"), 5)
                for r0 in range(0, NR, per):
                    bank = px[:, 2 + r0 * nk // 512, :]
                    M(bank, ident, bias_p[:, NR * g + r0:NR * g + r0 + per, SEQ - nk:SEQ], start=True, stop=False)
                    M(bank, C["bigI"], sc[:, tt, 0:nk].unsqueeze(1).broadcast_to([P, per, nk]), start=False, stop=False)
                    for r in range(per):
                        ins = M(bank[:, r * nk:(r + 1) * nk], proj[:, NR * g + r0 + r, P * tt:P * tt + P],
                                proj[:, ROW_K + g, 0:nk], start=False, stop=r == per - 1)
                ins.then_inc(S("lg_ready"), 1)

            def transpose(u):
                tt, nk = u // 2, P * (u // 2 + 1)
                pe.wait_ge(S("p_ready"), u + 1)
                pe.wait_ge(S("pt_ready") if u else S("vnat_ready"), max(u, 1))
                for s in range(tt + 1):
                    for r in range(NR):
                        ins = tr(px[:, 4 + s, P * r:P * r + P], prob[:, r * nk + P * s:r * nk + P * s + P], ident)
                ins.then_inc(S("pt_mm"), 1)

            def mix(u):
                tt, g = u // 2, u % 2
                pe.wait_ge(S("pt_ready"), u + 1)
                for s in range(tt + 1):
                    ins = M(px[:, 2, :], vnat[:, s, g * HD:(g + 1) * HD], pt[:, NR * P * s:NR * P * (s + 1)],
                            start=s == 0, stop=s == tt)
                ins.then_inc(S("mix_mm"), 1)

            def gate(_):
                pe.wait_ge(S("wgb_loaded"), 16)
                pe.wait_ge(S("norm_root"), 5)
                for r in range(2):
                    ins = M(px[:, r, 0:T], wgb[GB0:GB0 + RANK, r * P:(r + 1) * P], proj[GB0:GB0 + RANK, ROW_MISC, :],
                            start=True, stop=True)
                ins.then_inc(S("gl_gate"), 1)

            def pairs(m):
                if m == 0:
                    return proj[:, ROW_QB:ROW_QB + 2, :], proj[:, ROW_KB:ROW_KB + 2, :]
                return qe[:, (m - 1) % 2], ke[:, (m - 1) % 2]

            def level(m):
                q_, k_ = pairs(m)
                if m:
                    pe.wait_ge(S("level_ready"), m)
                    pe.wait_ge(S("level_read"), m)
                else:
                    pe.wait_ge(S("la_ready"), 1)
                    pe.wait_ge(S("qb_scaled"), 1)
                for tt in range(1 if m == 1 else 2):
                    tq = 1 if m == 1 else tt
                    for r in range(2):
                        for e in range(2):
                            pp = slice(64 * e, 64 * e + 64)
                            ins = M(px[:, e, 256 * tt + P * r:256 * tt + P * r + P], k_[pp, r, P * tt:P * tt + P],
                                    q_[pp, r, P * tq:P * tq + P], start=True, stop=True)
                ins.then_inc(S("level_mm"), 1)

            def level_s(_):
                pe.wait_ge(S("level_read"), 9)
                for n, m in enumerate((0, 7, 8)):
                    q_, k_ = pairs(m)
                    for r in range(2):
                        for e in range(2):
                            pp = slice(64 * e, 64 * e + 64)
                            ins = M(px[0:TS, e, TS * (2 * n + r):TS * (2 * n + r) + TS], k_[pp, r, SEQ:T], q_[pp, r, SEQ:T],
                                    start=True, stop=True)
                ins.then_inc(S("level_s_mm"), 1)

            def vn_nat(_):
                pe.wait_ge(S("norm_done"), 7)
                pe.wait_ge(S("mix_out"), 4)
                for tt, w in enumerate(widths):
                    for g in range(4):
                        ins = tr(px[0:w, [4, 5, 3][tt], P * g:P * g + P], proj[:, ROW_VC + g, P * tt:P * tt + w], ident)
                ins.then_inc(S("vn_mm"), 1)

            def vb_nat(_):
                pe.wait_ge(S("vnn_ready"), 1)
                for tt, w in enumerate(widths):
                    for q in range(BH):
                        ins = tr(px[0:w, [0, 1, 4][tt], P * q:P * q + P], proj[:, ROW_VB + q, P * tt:P * tt + w], ident)
                ins.then_inc(S("vb_mm"), 1)

            def softmax_s(x):
                pe.wait_ge(S("sel_s_ready"), 1)
                pe.wait_ge(S("keys_s_ready"), 1)
                out = px[:, 2 + x, 0:T]
                M(out, C["ex"][:, P * x:P * x + P], sc_s[:, 0:T], start=True, stop=False)
                M(out, C["eb"], bias_s[:, :], start=False, stop=False)
                for b4 in range(4):
                    pe.wait_ge(S(f"k_page{b4}"), 32 * (x + 1))
                    for g in range(NG):
                        ins = M(out[32 * b4:32 * b4 + 32, :], qpad[:, 4 * x + b4, g, :], k_s[:, b4, g, :],
                                start=False, stop=g == NG - 1)
                ins.then_inc(S("lg_s"), 1)

            def transpose_s(x):
                pe.wait_ge(S("p_s_ready"), x + 1)
                pe.wait_ge(S("pt_s_ready") if x else S("kdn_ready"), 1)
                for s, w in enumerate(widths):
                    ins = tr(px[0:w, 5, P * s:P * s + P], prob_s[:, x, P * s:P * s + w], ident)
                ins.then_inc(S("pt_s_mm"), 1)

            def mix_s(x):
                pe.wait_ge(S("pt_s_ready"), x + 1)
                for b4 in range(4):
                    pe.wait_ge(S(f"v_page{b4}"), 32 * (x + 1))
                    for g in range(NG):
                        col = 64 * g + 16 * b4
                        for s, w in enumerate(widths):
                            v = vnat[0:TS, 2, g * HD:(g + 1) * HD] if s == 2 else v_s[:, b4, s, g * HD:(g + 1) * HD]
                            pr = pt_s[0:w, x, P * s + 32 * b4:P * s + 32 * b4 + 32].rearrange("p (t h) -> p t h", h=NH)
                            ins = M(px[:, 2 + x, col:col + 16], v, pr[:, :, NR * g:NR * g + NR], start=s == 0, stop=s == 2)
                ins.then_inc(S("pv_s_mm"), 1)

            def kd_nat(_):
                pe.wait_ge(S("kd_ready"), 1)
                pe.wait_ge(S("vbn_ready"), 1)
                for tt, w in enumerate(widths):
                    for r in range(2):
                        dst = px[0:w, 5, 256 * tt + P * r:256 * tt + P * r + P] if tt < 2 else px[0:w, 4, P * r:P * r + P]
                        ins = tr(dst, kdT[:, r, P * tt:P * tt + w], ident)
                ins.then_inc(S("kd_mm"), 1)

            def quad(q):
                return acc[:, q, :] if q < 2 else px[:, q - 2, :]

            def outputs(_):
                pe.wait_ge(S("acc_read"), N_IN)
                pe.wait_ge(S("s0_loaded"), 16)
                for r in range(2):
                    for e in range(2):
                        hd, pp = 2 * r + e, slice(64 * e, 64 * e + 64)
                        vs = slice(BDV * hd, BDV * hd + BDV)
                        M(quad(hd)[:, 0:P], vbn[:, 0, vs], att[:, e, r, :], start=True, stop=True)
                        M(quad(hd)[:, P:SEQ], vbn[:, 0, vs], att_c[:, e, r, :], start=True, stop=False)
                        M(quad(hd)[:, P:SEQ], vbn[:, 1, vs], att[:, e, 2 + r, :], start=False, stop=True)
                        M(quad(hd)[:, SEQ:T], vbn[0:TS, 2, vs], att_s[:, e, TS * r:TS * r + TS], start=True, stop=False)
                        for b in range(NB):
                            ins = M(quad(hd)[:, SEQ + NS * b:SEQ + NS * b + NS], s0[pp, b, r, :],
                                    qes[pp, r, NS * b:NS * b + NS], start=False, stop=b == NB - 1)
                ins.then_inc(S("o_mm"), 1)

            def state_p(_):
                pe.wait_ge(S("kdn_ready"), 1)
                for r in range(2):
                    for e in range(2):
                        hd = 2 * r + e
                        for tt in range(2):
                            ins = M(px[64 * e:64 * e + 64, 4, P * r:P * r + P], kdn[:, tt, 64 * hd:64 * hd + 64],
                                    vbn[:, tt, BDV * hd:BDV * hd + BDV], start=tt == 0, stop=tt == 1)
                ins.then_inc(S("sp_mm"), 1)

            def out_norm(_):
                pe.wait_ge(S("osq_ready"), 1)
                for q in range(BH):
                    ins = M(quad(q)[:, 0:T], ones[:, :], osq[:, q, :], start=True, stop=True)
                ins.then_inc(S("o_ssq"), 1)

            def state_s(_):
                pe.wait_ge(S("o_root"), 1)
                pe.wait_ge(S("kdm_ready"), 1)
                for b in range(NB):
                    for r in range(2):
                        for e in range(2):
                            hd, place = 2 * r + e, 2 * b + r
                            ins = M(quad(place // 4)[64 * e:64 * e + 64, P * (place % 4):P * (place % 4) + P],
                                    kdm[:, b, 64 * hd:64 * hd + 64], vbn[0:TS, 2, BDV * hd:BDV * hd + BDV],
                                    start=True, stop=True)
                ins.then_inc(S("ss_mm"), 1)

            def spatial(_):
                pe.wait_ge(S("state_s_ready"), 1)
                pe.wait_ge(S("ws_ready"), 1)
                for g in range(4):
                    cs = slice(P * g, P * g + P)
                    for tt in range(2):
                        M(quad(g)[:, P * tt:P * tt + P], vnn[:, tt, cs], ws[:, g, :], start=True, stop=True)
                    ins = M(quad(g)[:, SEQ:T], vnn[0:TS, 2, cs], wss[:, g, :], start=True, stop=True)
                ins.then_inc(S("sp_gm"), 1)

            stages = dict(weights=weights, index=index, index_s=index_s, index_end=lambda _: index_sum(NB - 1),
                          norm=norm, values=values, softmax=softmax, transpose=transpose, mix=mix, gate=gate,
                          level=level, level_s=level_s, vn_nat=vn_nat, vb_nat=vb_nat, softmax_s=softmax_s,
                          transpose_s=transpose_s, mix_s=mix_s, kd_nat=kd_nat, outputs=outputs, state_p=state_p,
                          out_norm=out_norm, state_s=state_s, spatial=spatial)
            for t in range(FIRST_ROWS, N_IN):
                tile_free("in", t // 2, 2, t % 2)
                group("in", t // 2, t % 2, acc[:, t % 2, 0:T], 0, KT, x_hi, x_lo)
                do(stages, t)
            do(stages, AFTER)

            pe.wait_ge(S("m_ready"), 4)
            with pe.Fori(0, N_OUT // 2) as i:
                for j in range(2):
                    tile_free("out", i, 2, j)
                    group("out", i, j, acc[:, j, 0:T], 0, KT, m_hi, m_lo)
            for hf in range(HALVES):
                if hf == 0:
                    pe.wait_ge(S("n_ready"), KT)
                    pe.wait_ge(S("ssq_added"), KT)
                    mean_squares(1)
                with pe.Fori(0, FH) as i:
                    for j in range(2):
                        tile_free(f"up{hf}", i, 2, j)
                        group(f"up{hf}", i, j, acc[:, j, 0:T], 0, KT, n_hi, n_lo)
                pe.wait_ge(S("a_ready"), FH * (hf + 1))
                with pe.Fori(0, N_OUT // 2) as i:
                    for j in range(2):
                        tile_free(f"down{hf}", i, 2, j)
                        for kk in range(2):
                            group(f"down{hf}", i * 2 + j, kk, acc[:, j, 0:T], kk * DK, DK, a_hi, a_lo,
                                  first=kk == 0, last=kk == 1)
            pe.wait_ge(S("n_ready"), 2 * KT)
            pe.wait_ge(S("ssq_added"), 2 * KT)
            mean_squares(2)
            pe.wait_ge(S("p_ready2"), 1)

            def ple(i, j):
                base = stream["ple"][0]
                tile_free("ple", i, 2, j)
                pe.wait_ge(S("w_lo_done"), i * 2 + (base + j + 1))
                products(acc[:, j, 0:T], j, 0, KT, n_hi, n_lo)
                products(px[:, j, 0:T], j, 0, GK - KT, p_hi, p_lo, at=KT).then_inc(S("w_used"), 1)

            for j in range(2):
                ple(0, j)
            with pe.Fori(1, N_OUT // 2) as i:
                for j in range(2):
                    pe.wait_ge(S("y_ready"), i * 2 + (j - 1))
                    ple(i, j)


SHAPES = {"yT": (P, KT, T), "kvT": (P, 4, T), "kiT": (ID, T), "gla_p": (P, 2, BDV), "gla_s": (P, NB, 2, BDV),
          "vn_s": (P, 4, TS)}


def tiles(w, kt):
    k, m = w.shape
    return np.ascontiguousarray(w.reshape(kt, P, m // P, P).transpose(2, 1, 0, 3).reshape(m // P, P, kt * P))


def kernel(**inputs):
    import concourse.bacc as bacc
    from concourse.bass_utils import run_bass_kernel_spmd

    x = {k: np.asarray(v) for k, v in inputs.items()}

    def featT(p, s, n):
        both = np.concatenate([p.reshape(SEQ, n * P), s.reshape(TS, n * P)])
        return np.ascontiguousarray(both.T.reshape(n, P, T).transpose(1, 0, 2))

    w = x["w_in"][0]
    edges = np.cumsum([0, NH * HD, NG * HD, NG * HD, IH * ID, ID, IH, BH * BDK, BH * BDK, BH * BDV, RANK,
                       BH * BDV, 4 * P, 4 * P])
    q, k, v, qi, ki, wi, qb, kb, vb, gb, rb, uc, vc = [w[:, s:e] for s, e in zip(edges, edges[1:])]
    misc = np.zeros((D, P), w.dtype)
    misc[:, 0:IH] = wi
    misc[:, GB0:GB0 + RANK] = gb
    w_in = np.concatenate([qi, ki, ki, misc, q, k, v, qb, kb, vb, vc, rb, uc], axis=1)
    gate, up = tiles(x["w_ffn_gate"][0], KT), tiles(x["w_ffn_up"][0], KT)
    down = x["w_ffn_down"][0].reshape(HALVES, 2, DK, P, N_OUT, P).transpose(0, 4, 1, 3, 2, 5)
    small = np.concatenate([x["q_norm_g"][0][:, None], x["k_norm_g"][0][:, None], x["g_out_b"][0][:, None],
                            x["b_gate_b"][0].reshape(2, P).T, x["g_v_c"][0].reshape(4, P).T], axis=1)
    w_sp = x["w_spatial"][0].transpose(2, 0, 1)
    arrays = {
        "xT": featT(x["x_prompt"], x["x_sample"], KT),
        "pT": featT(x["p_prompt"], x["p_sample"], PLE // P),
        "gains": np.stack([x[g][0].reshape(KT, P).T for g in ("g_mix", "g_ffn", "g_ple")], axis=1),
        "small": small,
        "pages": x["page_table"].reshape(1, NB * NPG).astype(np.int32),
        "w_in": tiles(w_in, KT),
        "w_out": tiles(x["w_out"][0], KT),
        "w_gu": np.stack([gate, up], axis=1).reshape(2 * FT, P, KT * P),
        "w_down": down.reshape(HALVES * N_OUT * 2, P, DK * P),
        "w_ple": np.concatenate([tiles(x["w_ple_gate"][0], KT), tiles(x["w_ple_proj"][0], PLE // P)], axis=2),
        "cache_k": x["cache_k"][0].transpose(0, 3, 2, 1),
        "cache_v": x["cache_v"][0].reshape(NPOOL, PAGE, NG * HD),
        "cache_ik": np.tile(x["cache_idx_k"][0].transpose(0, 2, 1), (1, 2, 1)),
        "state": x["state_gla"][0].reshape(NB, 2, 2, BDK, BDV).transpose(2, 3, 0, 1, 4).reshape(P, NB, 2, BDV),
        "rel_bias": x["rel_bias"],
        "w_gate_b": x["w_gate_b"][0],
        "w_sp": w_sp,
        "w_sps": np.tile(w_sp[0:NS, :, 0:NS], (NB, 1, NB)),
        "b_sp": x["b_spatial"][0].reshape(4 * P),
        "consts": constants(),
    }
    arrays = {k_: np.ascontiguousarray(v_) for k_, v_ in arrays.items()}
    nc = bacc.Bacc("TRN2", target_bir_lowering=False, num_devices=1)
    a = {n: nc.dram_tensor(f"in_{n}", z.shape, mybir.dt.from_np(z.dtype), kind="ExternalInput").ap()
         for n, z in arrays.items()}
    o = {n: nc.dram_tensor(f"out_{n}", s, F32, kind="ExternalOutput").ap() for n, s in SHAPES.items()}
    build_layer(nc, a, o)
    r = run_bass_kernel_spmd(nc, [{f"in_{n}": z for n, z in arrays.items()}], core_ids=[0])
    y, kv, kiT, gp, gs, vn = [np.asarray(r.results[0][f"out_{n}"]) for n in SHAPES]
    y = y.transpose(2, 1, 0).reshape(T, D)
    kv = kv.transpose(2, 1, 0)
    kk, vv, ki_ = kv[:, 0:2], kv[:, 2:4], kiT.T

    def states(z, n):
        return z.reshape(2, BDK, n, 2, BDV).transpose(2, 3, 0, 1, 4).reshape(1, n, BH, BDK, BDV)

    return (y[:SEQ].reshape(1, SEQ, D), y[SEQ:].reshape(NB, NS, D),
            kk[:SEQ].reshape(1, 1, SEQ, NG, HD), vv[:SEQ].reshape(1, 1, SEQ, NG, HD),
            ki_[:SEQ].reshape(1, 1, SEQ, ID), states(gp, 1),
            kk[SEQ:].reshape(1, NB, NS, NG, HD), vv[SEQ:].reshape(1, NB, NS, NG, HD),
            ki_[SEQ:].reshape(1, NB, NS, ID), states(gs, NB),
            vn.transpose(2, 1, 0).reshape(1, NB, NS, 4 * P))
```

```python
from contextlib import ExitStack, contextmanager

import numpy as np

import concourse.bass as bass
from concourse import mybir

F32 = mybir.dt.float32
F32R = mybir.dt.float32r
I32 = mybir.dt.int32
U32 = mybir.dt.uint32
ALU = mybir.AluOpType
ACT = mybir.ActivationFunctionType
AX = mybir.AxisListType

P = 128
D = 2048
KT = D // P
SEQ, NB, NS = 256, 8, 4
TS = NB * NS
T = SEQ + TS
HD, NH, NG = 128, 8, 2
NR = NH // NG
IH, ID = 16, 64
PAST, PAGE, NPOOL = 256, 128, 20
NPG = PAST // PAGE
KSEL_P, KSEL_S = 64, 65
BH, BDK, BDV, RANK = 4, 64, 128, 16
FF, PLE = 5632, 256
EPS = 1e-6
GATE_TEMP = 16.0
NBUCKET, MAXDIST = 32, 128

ROW_Q, ROW_RB, ROW_UC, ROW_K, ROW_V, ROW_QI, ROW_KI, ROW_MISC = 0, 8, 12, 16, 18, 20, 28, 29
ROW_QB, ROW_KB, ROW_VB, ROW_VC = 30, 32, 34, 38
N_IN = 42
FIRST_ROWS = 10
ORDER = (*range(ROW_QI, ROW_QI + FIRST_ROWS), *range(ROW_Q, ROW_Q + 8), *range(ROW_K, ROW_K + 4),
         *range(ROW_QB, ROW_QB + 12), *range(ROW_RB, ROW_RB + 4), *range(ROW_UC, ROW_UC + 4))
GB0 = 32
N_OUT = D // P
FT = FF // P
HALVES = 2
FH = FT // HALVES
DK = FH // 2
GK = KT + PLE // P

NEG, MARK, TOP, BIG = -3.0e38, float(np.float32(-3.39e38)), 3.0e38, 1.0e30
DMAX = PAST + NS - 1
NDIST = 388
LEVELS = [64, 32, 16, 8, 4, 2, 1]
NORMS = [(ROW_Q, 0), (ROW_Q + 2, 0), (ROW_Q + 4, 0), (ROW_Q + 6, 0), (ROW_K, 1), (ROW_VC, 5), (ROW_VC + 2, 7)]

TIMETABLE = {
    10: [("weights", 0), ("bias_table", 0)],
    11: [("bias_out", 0), ("index", 0), ("index_s", 0), ("index", 1), ("index_s", 1)],
    12: [("index", 2), ("index_s", 2), ("index", 3), ("index_s", 3)],
    13: [("bias_in", 0), ("index", 4), ("index_s", 4), ("index", 5), ("index_s", 5)],
    14: [("index", 6), ("index_s", 6), ("index", 7), ("index_s", 7)],
    15: [("index_end", 0)],
    16: [("norm", 0), ("pick_s", (0, 2))],
    17: [("norm", 1), ("pick_s", (2, 5))],
    18: [("pick_s", (5, 8))],
    19: [("norm", 2), ("pick_s", (8, 9)), ("pick", (0, 0, 2))],
    20: [("norm", 3), ("pick", (0, 2, 5))],
    21: [("norm", 4), ("pick", (0, 5, 8))],
    22: [("gate", 0), ("values", 0), ("store_kv", 0), ("keys_s", 0)],
    23: [("softmax_s", 0), ("softmax", 0)],
    24: [("transpose_s", 0), ("transpose", 0), ("pick", (1, 0, 3))],
    25: [("mix_s", 0), ("mix", 0), ("softmax", 1), ("pick", (1, 3, 5))],
    26: [("softmax_s", 1), ("transpose", 1), ("scan", 0)],
    27: [("transpose_s", 1), ("mix", 1), ("pick", (1, 5, 8))],
    28: [("mix_s", 1), ("level", 0), ("softmax", 2)],
    29: [("transpose", 2), ("level", 1)],
    30: [("mix", 2), ("level", 2)],
    31: [("level", 3), ("softmax", 3)],
    32: [("transpose", 3), ("level", 4)],
    33: [("mix", 3), ("level", 5)],
    34: [("gelu_v", 0), ("norm", 5), ("level", 6)],
    35: [("norm", 6), ("level", 7), ("last", 0)],
    36: [("level", 8), ("decayed", 0), ("vn_nat", 0)],
    37: [("level_s", 0), ("vb_nat", 0), ("kd_nat", 0)],
    38: [("spatial", 0)],
    39: [("gate_rows", 0), ("outputs", 0), ("state_p", 0), ("gelu_u", 0)],
    40: [("out_norm", 0), ("state_s", 0), ("gelu_u", 1), ("gelu_u", 2)],
}


CONST = {"ident": (P, P), "bigI": (P, P), "lev": (P, 7 * P), "tril": (P, P), "wsm": (TS, TS),
         "scan": (P, T), "e16": (IH, 64), "wbm": (64, NB * TS), "adm": (TS, TS), "admneg": (TS, TS),
         "ex": (TS, 2 * P), "eb": (TS, P), "blk": (TS, NB), "bucket": (NBUCKET, NDIST)}


def const_columns():
    at, out = 0, {}
    for name, (rows, cols) in CONST.items():
        out[name] = (rows, at, cols)
        at += cols
    return out, at


def constants():
    where, total = const_columns()
    c = np.zeros((P, total), np.float32)

    def put(name, a):
        rows, at, cols = where[name]
        c[:rows, at:at + cols] = np.asarray(a, np.float32).reshape(rows, cols)

    p = np.arange(P)
    put("ident", np.eye(P))
    put("bigI", np.eye(P) * BIG)
    s, t = p[:, None], p[None, :]
    put("lev", np.stack([(s // (2 * L) == t // (2 * L)) & (s % (2 * L) < L) & (t % (2 * L) >= L)
                         for L in LEVELS], 1))
    put("tril", s <= t)
    b, i = np.arange(TS) // NS, np.arange(TS) % NS
    same = b[:, None] == b[None, :]
    put("wsm", same & (i[:, None] <= i[None, :]))
    scan = np.ones((P, T))
    scan[:, 0] = 0
    scan[:, SEQ::NS] = 0
    put("scan", scan)
    e, j, tq = np.arange(64) // 32, np.arange(64) % 32 // NS, np.arange(64) % NS
    put("e16", np.arange(IH)[:, None] == (2 * j + e)[None, :])
    put("wbm", ((b[None, None, :] == np.arange(NB)[None, :, None]) & (i[None, None, :] == tq[:, None, None]))
        * (ID ** -0.5 * IH ** -0.5))
    adm = same & (i[None, :] <= i[:, None])
    put("adm", adm)
    put("admneg", np.where(adm, 0.0, NEG))
    rb, rt, rh = np.arange(P) // 32, np.arange(P) % 32 // NH, np.arange(P) % NH
    put("ex", np.stack([(b[:, None] == (4 * x + rb)[None, :]) & (i[:, None] == rt[None, :])
                        for x in range(2)], 1) * BIG)
    put("eb", np.arange(32)[:, None] == (rt * NH + rh)[None, :])
    put("blk", b[:, None] == np.arange(NB)[None, :])
    dist = np.maximum(DMAX - np.arange(NDIST), 0)
    half = NBUCKET // 2
    large = half + (np.log(np.maximum(dist, 1).astype(np.float32) / half)
                    / np.float32(np.log(MAXDIST / half)) * (NBUCKET - half)).astype(np.int32)
    bucket = np.where(dist < half, dist, np.minimum(large, NBUCKET - 1))
    put("bucket", np.arange(NBUCKET)[:, None] == bucket[None, :])
    return c


class Steps:

    def __init__(self, eng, sem):
        self.eng, self.sem, self.n = eng, sem, 0

    def __call__(self, ins):
        self.n += 1
        ins.then_inc(self.sem, 1)
        self.eng.wait_ge(self.sem, self.n)

    @contextmanager
    def each(self, i, count, per):
        base, k = self.n, [0]

        def link(ins):
            k[0] += 1
            ins.then_inc(self.sem, 1)
            self.eng.wait_ge(self.sem, i * per + (base + k[0]))

        yield link
        assert k[0] == per, (k[0], per)
        self.n = base + per * count


def build_layer(nc, a, o):
    es = ExitStack()
    with es:
        def sb(name, shape, dt=F32, ctx=es):
            return ctx.enter_context(nc.sbuf_tensor(name, shape, dt))

        sems = {}

        def S(name):
            if name not in sems:
                sems[name] = es.enter_context(nc.semaphore(name))
            return sems[name]

        RW = GK * P
        raw = sb("w_raw", [P, 2, RW])
        whi = sb("w_hi", [P, 2, RW], F32R)
        wlo = sb("w_lo", [P, 2, RW], F32R)
        ones = sb("ones", [P, P])
        rstd = sb("rstd", [P, T])
        ssq = sb("ssq", [P, T])
        sqt = sb("sqt", [P, T])
        gains = sb("gains", [P, 3, KT])
        small = sb("small", [P, 16])
        pages = sb("pages", [1, NB * NPG], I32)
        tmp = sb("tmp", [P, 3, T])
        tmp1, tmp2, tmp3 = tmp[:, 0, :], tmp[:, 1, :], tmp[:, 2, :]
        epsc = sb("epsc", [P, 1])

        x_hi = sb("x_hi", [P, KT, T], F32R)
        x_lo = sb("x_lo", [P, KT, T], F32R)
        m_hi, m_lo = x_hi, x_lo

        proj_ctx = ExitStack()
        proj = sb("proj", [P, N_IN, T], ctx=proj_ctx)
        where, n_const = const_columns()
        consts = sb("consts", [P, n_const], ctx=proj_ctx)
        C = {n: consts[0:r, at:at + cols] for n, (r, at, cols) in where.items()}
        bias_p = sb("bias_p", [P, NH, SEQ], ctx=proj_ctx)
        bias_s = sb("bias_s", [TS, T], ctx=proj_ctx)
        bias_n = sb("bias_n", [TS, NS], ctx=proj_ctx)
        vnat = sb("vnat", [P, 3, NG * HD], ctx=proj_ctx)
        wi_n = sb("wi_n", [P, 2, IH], ctx=proj_ctx)
        sc = sb("sc", [P, 2, SEQ], ctx=proj_ctx)
        top8 = sb("top8", [P, 8], ctx=proj_ctx)
        sc_s = sb("sc_s", [TS, T + 7], ctx=proj_ctx)
        top8s = sb("top8s", [TS, 8], ctx=proj_ctx)
        sm = sb("sm", [P, 20], ctx=proj_ctx)
        wgb = sb("wgb", [P, 256], ctx=proj_ctx)
        lg2 = sb("lg2", [P, 4, T], ctx=proj_ctx)
        la, lsp = lg2[:, 0:2, :], lg2[:, 2:4, :]
        bc = sb("bc", [P, 2, T], ctx=proj_ctx)
        dd = sb("dd", [P, 2, 2, T], ctx=proj_ctx)
        ebs = sb("ebs", [P, 2, TS], ctx=proj_ctx)
        qes = sb("qes", [P, 2, NB, 2, NS], ctx=proj_ctx)
        att = sb("att", [P, 2, 4, P], ctx=proj_ctx)
        att_c = sb("att_c", [P, 2, 2, P], ctx=proj_ctx)
        att_s = sb("att_s", [TS, 2, 2 * TS], ctx=proj_ctx)
        ix_ctx = ExitStack()
        rl = sb("rl", [P, 4, SEQ], ctx=ix_ctx)
        ki_s = sb("ki_s", [P, 2, T], ctx=ix_ctx)
        rl_s = sb("rl_s", [64, 2, T], ctx=ix_ctx)
        wb = sb("wb", [64, NB, TS], ctx=ix_ctx)
        qi_s = sb("qi_s", [P, NB, 32], ctx=ix_ctx)
        btab = sb("btab", [NH, NDIST], ctx=ix_ctx)
        relb = sb("relb", [NBUCKET, NH], ctx=ix_ctx)
        ix_ctx.close()
        soft = sb("soft", [P, 2 * NR * SEQ + NB * NG * 32], ctx=proj_ctx)
        sp_o = sb("sp_o", [P, 2, BDV], ctx=proj_ctx)
        proj_ctx.close()
        x_f = proj[:, 0:KT, :]
        qk = proj[:, ROW_QI:ROW_QI + 8, :].rearrange("p (z n r) t -> p z n r t", z=2, n=2)
        qe, ke = qk[:, 0], qk[:, 1]
        kdm = proj[0:TS, ROW_QI:ROW_QI + 8, :].rearrange("p a t -> p (a t)")[:, 0:NB * 256]\
            .rearrange("p (b n) -> p b n", b=NB)
        prob, pt = soft[:, 0:NR * SEQ], soft[:, NR * SEQ:2 * NR * SEQ]
        prob_s, pt_s = prob[:, NR * P:NR * P + T], pt[:, NR * P:NR * P + 3 * P]
        qpad = soft[:, 2 * NR * SEQ:2 * NR * SEQ + NB * NG * 32].rearrange("p (b g n) -> p b g n", b=NB, g=NG)
        vbn = soft[:, 0:3 * 512].rearrange("p (a n) -> p a n", a=3)
        kdn = soft[:, 3 * 512:3 * 768].rearrange("p (a n) -> p a n", a=3)

        def rows(first, last):
            return proj[:, first:last, :].rearrange("p a t -> p (a t)")

        k_s = rows(ROW_QI, ROW_QI + 8).rearrange("p (b g t) -> p b g t", b=4, g=NG)
        v_s = rows(ROW_RB, ROW_RB + 8)[:, 0:8 * NG * HD].rearrange("p (b n d) -> p b n d", b=4, n=NPG)
        s0 = [rows(r, r + 4)[:, 0:8 * BDV].rearrange("p (b r v) -> p b r v", b=4, r=2) for r in (ROW_K, ROW_VC)]
        sqb = tmp[:, 0:2, :]
        kdT = tmp[:, 0:2, :]
        ob = dd[:, :, :, :].rearrange("p a r t -> p (a r) t")
        osq = lg2[:, :, :]
        gsum = proj[:, ROW_VB:ROW_VB + 4, :]
        vnn = bias_p[:, 0:6, :].rearrange("p a b -> p (a b)").rearrange("p (a b) -> p a b", a=3)
        flat = lg2[:, :, :].rearrange("p a t -> p (a t)")
        ws = flat[:, 0:4 * P].rearrange("p (g t) -> p g t", g=4)
        bsp = flat[:, 4 * P:8 * P].rearrange("p (g t) -> p g t", g=4)
        wss = flat[0:TS, 8 * P:8 * P + 4 * TS].rearrange("p (g t) -> p g t", g=4)
        n_hi = sb("n_hi", [P, KT, T], F32R)
        h = sb("h", [P, KT, T])
        n_lo = sb("n_lo", [P, KT, T], F32R)
        a_hi = sb("a_hi", [P, FH, T], F32R)
        a_lo = sb("a_lo", [P, FH, T], F32R)
        p_f = sb("p_f", [P, 2, T])
        p_hi = m_hi[:, 2:4, :]
        p_lo = m_lo[:, 0:2, :]

        acc = es.enter_context(nc.psum_tensor("acc", [P, 2, 512], F32))
        px = es.enter_context(nc.psum_tensor("px", [P, 6, 512], F32))
        table = nc.dram_tensor("bias_table", [NH, P, NDIST], F32, kind="Internal").ap()

        phases = [("in", N_IN, KT, a["w_in"], 0), ("out", N_OUT, KT, a["w_out"], 0)]
        for hf in range(HALVES):
            phases += [(f"up{hf}", 2 * FH, KT, a["w_gu"], hf * 2 * FH),
                       (f"down{hf}", 2 * N_OUT, DK, a["w_down"], hf * 2 * N_OUT)]
        phases += [("ple", N_OUT, GK, a["w_ple"], 0)]
        stream, g0 = {}, 0
        for name, n, kt, src, first in phases:
            stream[name] = (g0, n, kt, src, first)
            g0 += n
        following = {x[0]: y[0] for x, y in zip(phases, phases[1:])}

        loaded = [S("w_loaded0"), S("w_loaded1")]

        def load_group(sp, name, i, j):
            base, n, kt, src, first = stream[name]
            G = base + j + i * 2
            if not isinstance(i, int) or G >= 2:
                sp.wait_ge(S("w_lo_done"), G - 1)
            row = src[bass.ds(i * 2 + (first + j), 1), :, :].rearrange("o p n -> (o p) n")
            sp.dma_start(raw[:, j, 0:kt * P], row).then_inc(loaded[j], 16)

        def load_phase(sp, name, done=0):
            base, n, kt, src, first = stream[name]
            for i in range(done // 2, 1 if base == 0 else done // 2):
                for j in range(2):
                    load_group(sp, name, i, j)
            with sp.Fori(max(done // 2, 1 if base == 0 else 0), n // 2) as i:
                for j in range(2):
                    load_group(sp, name, i, j)

        def split_hi(act, name, i, j):
            base, n, kt, src, first = stream[name]
            G = base + j + i * 2
            act.wait_ge(loaded[j], i * 16 + (base // 2 * 16 + 16))
            if not isinstance(i, int) or G >= 2:
                act.wait_ge(S("w_used"), G - 1)
            nc.scalar.activation(whi[:, j, 0:kt * P], raw[:, j, 0:kt * P], ACT.Copy).then_inc(S("w_hi_done"), 1)

        def split_lo(dve, name, i, j):
            base, n, kt, src, first = stream[name]
            G = base + j + i * 2
            dve.wait_ge(S("w_hi_done"), G + 1)
            nc.vector.tensor_tensor(wlo[:, j, 0:kt * P], raw[:, j, 0:kt * P], whi[:, j, 0:kt * P].bitcast(F32),
                                    ALU.subtract).then_inc(S("w_lo_done"), 1)

        def paced(eng, name, split, evict, start=0):
            base, n, *_ = stream[name]
            if n > 2:
                with eng.Fori(start, n // 2 - 1) as i:
                    split(eng, name, i, 1)
                    evict(i, 0)
                    split(eng, name, i + 1, 0)
                    evict(i, 1)
            i = n // 2 - 1
            split(eng, name, i, 1)
            evict(i, 0)
            if name in following:
                split(eng, following[name], 0, 0)
            evict(i, 1)

        def products(out, j, k0, kt, m_hi_, m_lo_, first=True, last=True, at=0):
            for k in range(kt):
                w_h = whi[:, j, (at + k) * P:(at + k + 1) * P]
                w_l = wlo[:, j, (at + k) * P:(at + k + 1) * P]
                nc.tensor.matmul(out, w_h, m_hi_[:, k0 + k, :], start=first and k == 0, stop=False)
                nc.tensor.matmul(out, w_h, m_lo_[:, k0 + k, :], start=False, stop=False)
                ins = nc.tensor.matmul(out, w_l, m_hi_[:, k0 + k, :], start=False, stop=last and k == kt - 1)
            return ins

        def out_s(r):
            return px[:, 4, 64 * r:64 * r + 64].rearrange("p (b e i) -> p b e i", b=NB, e=2)

        block = es.enter_context(nc.Block())

        widths = [P, P, TS]

        tile0, n_tiles = {}, 0
        for name, n, *_ in phases:
            tile0[name] = n_tiles
            n_tiles += n // 2 if name.startswith("down") else n

        def kept(row):
            return ORDER.index(row) + 1

        def do(stages, slot):
            for stage, arg in TIMETABLE.get(slot, ()) if isinstance(slot, int) else slot:
                if stage in stages:
                    stages[stage](arg)

        levels = [P] + LEVELS

        def by_seq(ap):
            return ap.rearrange("p r (b i) -> p r b i", i=NS)

        def blocks(ap, n):
            L, w = levels[n], (T if levels[n] <= NS // 2 else SEQ)
            v = ap[:, :, 0:w].rearrange("p r (b l) -> p r b l", l=2 * L)
            return v[:, :, :, 0:L], v[:, :, :, L:2 * L], w // (2 * L), L

        @block.sync
        def _(sp):
            sp.dma_start(gains[:, :, :], a["gains"]).then_inc(S("small_loaded"), 16)
            for c in range(4):
                sp.dma_start(x_f[:, 4 * c:4 * c + 4, :], a["xT"][:, 4 * c:4 * c + 4, :]).then_inc(S(f"x_loaded{c}"), 16)
                sp.dma_start(raw[:, 0, 4 * c * P:4 * (c + 1) * P], a["w_in"][0, :, 4 * c * P:4 * (c + 1) * P])\
                    .then_inc(loaded[0] if c == 3 else S(f"w_quarter{c}"), 16)
            load_group(sp, "in", 0, 1)
            sp.dma_start(small[:, 0:9], a["small"]).then_inc(S("small_loaded"), 16)
            sp.dma_start(consts[:, :], a["consts"]).then_inc(S("consts_loaded"), 16)
            sp.dma_start(relb[:, :], a["rel_bias"]).then_inc(S("consts_loaded"), 16)
            sp.dma_start(wgb[GB0:GB0 + RANK, :], a["w_gate_b"]).then_inc(S("wgb_loaded"), 16)
            load_phase(sp, "in", done=2)
            for j in range(2):
                load_group(sp, "out", 0, j)
            load_phase(sp, "out", done=2)
            for hf in range(HALVES):
                load_phase(sp, f"up{hf}")
                if hf == 0:
                    sp.dma_start(p_f[:, :, :], a["pT"]).then_inc(S("p_loaded"), 16)
                load_phase(sp, f"down{hf}")
            load_phase(sp, "ple")
            for m0, m1 in ((0, 8), (8, 12), (12, 14), (14, 16)):
                sp.wait_ge(S("y_ready"), m1)
                sp.dma_start(o["yT"][:, m0:m1, :], h[:, m0:m1, :]).then_inc(S("y_stored"), 16)
            sp.wait_ge(S("y_stored"), 16 * 4)

        @block.gpsimd
        def _(pool):
            link = Steps(pool, S("pool_step"))
            nc.gpsimd.memset(epsc[:, :], EPS)
            nc.gpsimd.memset(ones[:, :], 1.0).then_inc(S("ones_ready"), 1)
            for c in range(4):
                pool.wait_ge(S(f"x_loaded{c}"), 16)
                xc = x_f[:, 4 * c:4 * c + 4, :]
                nc.gpsimd.tensor_tensor(proj[:, KT + 4 * c:KT + 4 * c + 4, :], xc, xc, ALU.mult).then_inc(S("x_sq"), 1)
            for n in (4, 2, 1):
                pool.wait_ge(S("x_sq"), 4)
                part = proj[:, KT + 8:KT + 8 + n, :]
                ins = nc.gpsimd.tensor_tensor(part, part, proj[:, KT + 8 + n:KT + 8 + 2 * n, :], ALU.add)
                link(ins) if n > 1 else ins.then_inc(S("x_half"), 1)
            nc.gpsimd.memset(att[:, :, :, :], 0.0)
            nc.gpsimd.memset(att_s[:, :, :], 0.0)
            nc.gpsimd.memset(sc_s[:, T:T + 7], TOP).then_inc(S("att_zero"), 1)
            nc.gpsimd.dma_start(pages[:, :], a["pages"]).then_inc(S("pages_loaded"), 16)
            pool.wait_ge(S("pages_loaded"), 16)

            def page(b, n):
                return pool.value_load(pages[0:1, b * NPG + n:b * NPG + n + 1], min_val=0, max_val=NPOOL - 1)

            def index_keys(b):
                if b >= 2:
                    pool.wait_ge(S("idx_s_mm"), b - 1)
                for n in range(NPG):
                    src = a["cache_ik"][bass.ds(page(b, n), 1), :, :].rearrange("o p n -> (o p) n")
                    pool.dma_start(ki_s[:, b % 2, n * PAGE:(n + 1) * PAGE], src).then_inc(S(f"ki_page{b % 2}"), 16)

            diag = [sc[:, 0, 0:P], sc[:, 1, P:SEQ]]

            def mask_scores(tt):
                pool.wait_ge(S("rl_free"), 4 * tt + 4)
                nc.gpsimd.affine_select(out=diag[tt], in_=diag[tt], compare_op=ALU.is_ge, fill=NEG, base=0,
                                        pattern=[[-1, P]], channel_multiplier=1).then_inc(S("scores_masked"), 1)

            def mask_choice(tt):
                pool.wait_ge(S("picked"), tt + 1)
                nc.gpsimd.affine_select(out=diag[tt], in_=diag[tt], compare_op=ALU.is_ge, fill=-1.0, base=0,
                                        pattern=[[-1, P]], channel_multiplier=1).then_inc(S("sel_ready"), 1)

            for b in range(6):
                index_keys(b)
            mask_scores(0)
            index_keys(6)
            index_keys(7)
            mask_scores(1)
            pool.wait_ge(S("idx_mm"), 8)
            pool.wait_ge(S("weights_done"), 1)
            pool.wait_ge(S("x_ready"), 4)
            pool.wait_ge(S("x_sq"), 4)
            for b in range(NB):
                if b == 4:
                    mask_choice(0)
                    pool.wait_ge(S("lg_s"), 1)
                for n in range(NPG):
                    pid = page(b, n)
                    pool.dma_start(k_s[:, b % 4, :, n * PAGE:(n + 1) * PAGE],
                                   a["cache_k"][bass.ds(pid, 1), :, :, :].rearrange("o p g n -> (o p) g n"))\
                        .then_inc(S(f"k_page{b % 4}"), 16)
                    if b < 4:
                        pool.dma_start(v_s[:, b % 4, n, :], a["cache_v"][bass.ds(pid, 1), :, :]
                                       .rearrange("o p n -> (o p) n")).then_inc(S(f"v_page{b % 4}"), 16)
            pool.wait_ge(S("pv_s_mm"), 1)
            for b in range(4, NB):
                for n in range(NPG):
                    pool.dma_start(v_s[:, b % 4, n, :], a["cache_v"][bass.ds(page(b, n), 1), :, :]
                                   .rearrange("o p n -> (o p) n")).then_inc(S(f"v_page{b % 4}"), 16)

            def distances(n):
                if n >= 2:
                    pool.wait_ge(S("level_ready"), n - 1)
                b1, b2, nb, L = blocks(bc, n)
                d1, d2, _, _ = blocks(dd[:, n % 2, :, :], n)
                mid = b1[:, :, :, L - 1:L].broadcast_to([P, 2, nb, L])
                nc.gpsimd.tensor_tensor(d1, mid, b1, ALU.subtract)
                nc.gpsimd.tensor_tensor(d2, b2, mid, ALU.subtract).then_inc(S("d_level"), 1)

            pool.wait_ge(S("scanned"), 1)
            distances(0)
            distances(1)
            mask_choice(1)
            pool.dma_start(ws, a["w_sp"]).then_inc(S("gm_loaded"), 16)
            pool.dma_start(wss, a["w_sps"]).then_inc(S("gm_loaded"), 16)
            pool.dma_start(bsp.rearrange("p g t -> p (g t)"), a["b_sp"].partition_broadcast(P)).then_inc(S("gm_loaded"), 16)
            distances(2)
            pool.wait_ge(S("gm_loaded"), 48)
            nc.gpsimd.tensor_tensor(ws, ws, C["tril"].unsqueeze(1).broadcast_to([P, 4, P]), ALU.mult)
            nc.gpsimd.tensor_tensor(wss, wss, C["wsm"].unsqueeze(1).broadcast_to([TS, 4, TS]), ALU.mult)\
                .then_inc(S("ws_ready"), 1)
            for n in range(3, 6):
                distances(n)
            pool.wait_ge(S("kv_stored"), 32)
            pool.wait_ge(S("lg_ready"), 4)
            pool.dma_start(s0[0], a["state"][:, 0:4, :, :]).then_inc(S("s0_loaded"), 16)
            distances(6)
            distances(7)
            pool.wait_ge(S("vn_stored"), 16)
            pool.wait_ge(S("vn_mm"), 1)
            pool.dma_start(s0[1], a["state"][:, 4:8, :, :]).then_inc(S("s0_loaded"), 16)
            pool.wait_ge(S("kdn_ready"), 1)
            pool.wait_ge(S("level_s_read"), 1)
            nc.gpsimd.tensor_tensor(kdm, kdn[0:TS, 2, :].unsqueeze(1).broadcast_to([TS, NB, 256]),
                                    C["blk"].unsqueeze(2).broadcast_to([TS, NB, 256]), ALU.mult).then_inc(S("kdm_ready"), 1)
            pool.wait_ge(S("state_p_ready"), 1)
            pool.dma_start(o["gla_p"], sp_o[:, :, :]).then_inc(S("state_stored"), 16)
            pool.wait_ge(S("state_s_ready"), 1)
            pool.dma_start(o["gla_s"][:, 0:4, :, :], s0[0]).then_inc(S("state_stored"), 16)
            pool.wait_ge(S("ss_mm"), 2)
            pool.wait_ge(S("kv_stored"), 32)
            pool.dma_start(h[:, 4:16, :], a["xT"][:, 4:16, :]).then_inc(S("h_loaded"), 16)
            pool.wait_ge(S("state_stored"), 16 * 2)
            pool.dma_start(h[:, 0:4, :], a["xT"][:, 0:4, :]).then_inc(S("h_loaded"), 16)
            pool.wait_ge(S("state_s_ready"), 2)
            pool.dma_start(o["gla_s"][:, 4:8, :, :], s0[1]).then_inc(S("state_stored"), 16)
            for nth, name in enumerate(["out", f"down{HALVES - 1}"]):
                pool.wait_ge(S("ms_mm"), nth + 1)
                link(nc.gpsimd.memset(ssq[:, :], 0.0))
                with pool.Fori(0, KT) as m, link.each(m, KT, 1) as lk:
                    pool.wait_ge(S("acc_read"), m + (tile0[name] + 1))
                    hm = h[:, bass.ds(m, 1), :].rearrange("p o t -> p (o t)")
                    lk(nc.gpsimd.tensor_tensor(sqt[:, :], hm, hm, ALU.mult))
                    nc.gpsimd.tensor_tensor(ssq[:, :], ssq[:, :], sqt[:, :], ALU.add).then_inc(S("ssq_added"), 1)
                    pool.wait_ge(S("ssq_added"), m + (nth * KT + 1))

        @block.scalar
        def _(act):
            link = Steps(act, S("act_step"))
            A = nc.scalar.activation

            def root(n):
                act.wait_ge(S("ms_mm"), n + 1)
                link(A(rstd[:, :], px[:, 5, 0:T], ACT.Ln, scale=1.0 / D, bias=epsc[:, 0:1]))
                A(rstd[:, :], rstd[:, :], ACT.Exp, scale=-0.5).then_inc(S("root_ready"), 1)

            act.wait_ge(S("small_loaded"), 16)
            for c in range(4):
                act.wait_ge(S(f"x_loaded{c}"), 16)
                for k in range(4 * c, 4 * c + 4):
                    ins = A(x_hi[:, k, :], x_f[:, k, :], ACT.Copy, scale=gains[:, 0, k:k + 1])
                ins.then_inc(S("x_hi_ready"), 1)
                act.wait_ge(loaded[0] if c == 3 else S(f"w_quarter{c}"), 16)
                A(whi[:, 0, 4 * c * P:4 * (c + 1) * P], raw[:, 0, 4 * c * P:4 * (c + 1) * P], ACT.Copy)\
                    .then_inc(S("w_hi_done") if c == 3 else S("w_quarter_hi"), 1)
            split_hi(act, "in", 0, 1)
            split_hi(act, "in", 1, 0)
            root(0)
            with act.Fori(1, FIRST_ROWS // 2) as i:
                for j in range(2):
                    split_hi(act, "in", i + j, 1 - j)

            def bias_out(_):
                act.wait_ge(S("btab_ready"), 1)
                act.dma_start(table, btab[:, :].unsqueeze(1).broadcast_to([NH, P, NDIST])).then_inc(S("table_written"), 16)

            def bias_in(_):
                act.wait_ge(S("table_written"), 16)
                for dst, first, rows, keys in ((bias_p[:, :, :], DMAX - P, P, SEQ), (bias_s[:, 0:PAST], DMAX - PAST, NS, PAST),
                                               (bias_n[:, :], DMAX, NS, NS)):
                    src = bass.AP(tensor=table.tensor, offset=first, ap=[[NDIST - 1, rows], [P * NDIST, NH], [1, keys]])
                    act.dma_start(dst, src).then_inc(S("bias_loaded"), 16)

            def index(st):
                nk = P * (st // 4 + 1)
                act.wait_ge(S("idx_mm"), st + 1)
                if st:
                    act.wait_ge(S("rl_free"), st)
                src = px[:, 0:2, :].rearrange("p e (j s) -> p e j s", j=2)[:, :, :, 0:nk]
                dst = rl[:, :, :].rearrange("p (e j) s -> p e j s", e=2)[:, :, :, 0:nk]
                A(dst, src, ACT.Relu).then_inc(S("relu_done"), 1)

            def index_s(b):
                act.wait_ge(S("idx_s_mm"), b + 1)
                if b >= 2:
                    act.wait_ge(S("idx_s_acc"), b - 1)
                for e in range(2):
                    pp = slice(32 * e, 32 * e + 32)
                    A(rl_s[pp, b % 2, :], px[pp, 4 + e, 0:T], ACT.Relu).then_inc(S("relu_s_done"), 1)

            def norm(n):
                row, _ = NORMS[n]
                bank = 0 if n < 5 else 2
                if n < 5:
                    act.wait_ge(S("acc_read"), kept(row + 1))
                if n:
                    act.wait_ge(S("norm_done"), n)
                A(sqb, proj[:, row:row + 2, :], ACT.Square).then_inc(S("norm_sq"), 1)
                act.wait_ge(S("norm_mm"), n + 1)
                link(A(sqb, px[:, bank:bank + 2, 0:T], ACT.Ln, scale=1.0 / P, bias=epsc[:, 0:1]))
                A(sqb, sqb, ACT.Exp, scale=-0.5).then_inc(S("norm_root"), 1)
                if n == 6:
                    act.wait_ge(S("norm_done"), 7)
                    act.dma_start(o["vn_s"], proj[:, ROW_VC:ROW_VC + 4, SEQ:T]).then_inc(S("vn_stored"), 16)

            def store_kv(_):
                act.wait_ge(S("norm_done"), 5)
                act.dma_start(o["kvT"][:, 0:4, :], proj[:, ROW_K:ROW_K + 4, :]).then_inc(S("kv_stored"), 16)
                act.dma_start(o["kiT"], proj[0:ID, ROW_KI, :]).then_inc(S("kv_stored"), 16)

            def values(_):
                act.wait_ge(S("values_mm"), 1)
                A(vnat[:, 0:2, :].rearrange("p a b -> p (a b)"), px[:, 4, :], ACT.Copy)
                A(vnat[0:TS, 2, :], px[0:TS, 5, 0:256], ACT.Copy).then_inc(S("vnat_ready"), 1)

            def softmax(u):
                nk = P * (u // 2 + 1)
                logits = px[:, 2:4, :].rearrange("p b s -> p (b s)")[:, 0:NR * nk].rearrange("p (r s) -> p r s", r=NR)
                act.wait_ge(S("max_ready"), u + 1)
                if u:
                    act.wait_ge(S("pt_mm"), u)
                for r in range(NR):
                    ins = A(prob[:, r * nk:(r + 1) * nk], logits[:, r, :], ACT.Exp, bias=sm[:, r:r + 1],
                            accum_out=sm[:, 4 + r:5 + r])
                ins.then_inc(S("exp_ready"), 1)

            def transpose(u):
                act.wait_ge(S("pt_mm"), u + 1)
                if u:
                    act.wait_ge(S("mix_mm"), u)
                tiles_ = u // 2 + 1
                A(pt[:, 0:tiles_ * NR * P].rearrange("p (a b) -> p a b", a=tiles_), px[:, 4:4 + tiles_, :], ACT.Copy)\
                    .then_inc(S("pt_ready"), 1)

            def mix(u):
                tt, g = u // 2, u % 2
                act.wait_ge(S("mix_mm"), u + 1)
                A(proj[:, NR * g:NR * g + NR, P * tt:P * tt + P], px[:, 2, :].rearrange("p (r t) -> p r t", r=NR),
                  ACT.Copy).then_inc(S("mix_out"), 1)

            def gate(_):
                act.wait_ge(S("la_ready"), 1)
                link(A(lsp, la, ACT.Abs))
                link(A(lsp, lsp, ACT.Exp, scale=-1.0))
                A(lsp, lsp, ACT.Ln, bias=1.0).then_inc(S("lsp_ready"), 1)

            def decays(n):
                act.wait_ge(S("d_level"), n + 1)
                w = T if n >= 6 else SEQ
                A(dd[:, n % 2, :, 0:w], dd[:, n % 2, :, 0:w], ACT.Exp, scale=1.0 / GATE_TEMP).then_inc(S("e_level"), 1)

            def last(_):
                act.wait_ge(S("d_last"), 1)
                A(dd[:, 1, :, :], dd[:, 1, :, :], ACT.Exp, scale=-1.0 / GATE_TEMP)
                A(ebs[:, :, :], bc[:, :, SEQ:T], ACT.Exp, scale=1.0 / GATE_TEMP).then_inc(S("e_last"), 1)

            def gelu_v(_):
                act.wait_ge(S("acc_read"), kept(ROW_VC + 3))
                link(A(proj[:, ROW_VC:ROW_VC + 4, :], proj[:, ROW_VC:ROW_VC + 4, :], ACT.Gelu_apprx_tanh))

            def gate_rows(_):
                act.wait_ge(S("acc_read"), kept(ROW_RB + 3))
                A(proj[:, ROW_RB:ROW_RB + 4, :], proj[:, ROW_RB:ROW_RB + 4, :], ACT.Silu).then_inc(S("silu_ready"), 1)

            def gelu_u(r):
                act.wait_ge(S("acc_read"), kept(ROW_UC + r))
                A(proj[:, ROW_UC + r, :], proj[:, ROW_UC + r, :], ACT.Gelu_apprx_tanh).then_inc(S("gelu_ready"), 1)

            def vn_nat(_):
                act.wait_ge(S("vn_mm"), 1)
                A(vnn[:, 0:2, :], px[:, 4:6, :], ACT.Copy)
                A(vnn[0:TS, 2, :], px[0:TS, 3, :], ACT.Copy).then_inc(S("vnn_ready"), 1)

            def vb_nat(_):
                act.wait_ge(S("vb_mm"), 1)
                A(vbn[:, 0:2, :], px[:, 2:4, :], ACT.Copy)
                A(vbn[0:TS, 2, :], px[0:TS, 4, :], ACT.Copy).then_inc(S("vbn_ready"), 1)

            def kd_nat(_):
                act.wait_ge(S("kd_mm"), 1)
                A(kdn[:, 0:2, :].rearrange("p a b -> p (a b)"), px[:, 5, :], ACT.Copy)
                A(kdn[0:TS, 2, :], px[0:TS, 0, 0:256], ACT.Copy).then_inc(S("kdn_ready"), 1)

            def softmax_s(x):
                act.wait_ge(S("max_s_ready"), x + 1)
                if x:
                    act.wait_ge(S("pt_s_mm"), x)
                A(prob_s, px[:, x, 0:T], ACT.Exp, bias=sm[:, 16:17], accum_out=sm[:, 17:18]).then_inc(S("exp_s_ready"), 1)

            def transpose_s(x):
                act.wait_ge(S("pt_s_mm"), x + 1)
                if x:
                    act.wait_ge(S("pv_s_mm"), x)
                A(pt_s[:, 0:2 * P], px[:, 5, 0:2 * P], ACT.Copy)
                A(pt_s[0:TS, 2 * P:3 * P], px[0:TS, 5, 2 * P:3 * P], ACT.Copy).then_inc(S("pt_s_ready"), 1)

            def outputs(_):
                act.wait_ge(S("o_mm"), 1)
                act.wait_ge(S("gsum_ready"), 1)
                A(ob[:, :, 0:SEQ], px[:, 0:4, 0:SEQ], ACT.Copy)
                for r in range(2):
                    ins = A(ob[:, 2 * r:2 * r + 2, SEQ:T].rearrange("p e (b i) -> p e b i", b=NB),
                            out_s(r).rearrange("p b e i -> p e b i"), ACT.Copy)
                link(ins)
                A(osq, ob, ACT.Square).then_inc(S("osq_ready"), 1)

            def state_p(_):
                act.wait_ge(S("sp_mm"), 1)
                A(sp_o[:, :, :].rearrange("p a b -> p (a b)"), px[:, 5, 0:256], ACT.Copy).then_inc(S("state_p_ready"), 1)

            def out_norm(_):
                act.wait_ge(S("o_ssq"), 1)
                link(A(osq, px[:, 0:4, 0:T], ACT.Ln, scale=1.0 / BDV, bias=epsc[:, 0:1]))
                A(osq, osq, ACT.Exp, scale=-0.5).then_inc(S("o_root"), 1)

            def level(m):
                if m + 1 < 8:
                    decays(m + 1)

            stages = dict(bias_out=bias_out, bias_in=bias_in, index=index, index_s=index_s, norm=norm, values=values, softmax=softmax,
                          transpose=transpose, mix=mix, gate=gate, scan=lambda _: decays(0), level=level, last=last,
                          gelu_v=gelu_v, gate_rows=gate_rows, vn_nat=vn_nat, vb_nat=vb_nat, kd_nat=kd_nat,
                          softmax_s=softmax_s, transpose_s=transpose_s, outputs=outputs, state_p=state_p,
                          out_norm=out_norm, store_kv=store_kv, gelu_u=gelu_u)
            for t in range(FIRST_ROWS, N_IN):
                if t + 1 < N_IN:
                    split_hi(act, "in", (t + 1) // 2, (t + 1) % 2)
                else:
                    split_hi(act, "out", 0, 0)
                do(stages, t)
            def part(c):
                A(m_hi[:, 4 * c:4 * c + 4, :], proj[:, 4 * c:4 * c + 4, :], ACT.Copy).then_inc(S("m_hi_ready"), 1)

            act.wait_ge(S("w_used"), N_IN)
            act.wait_ge(S("mix_s_out"), 2)
            part(0)
            part(1)
            act.wait_ge(S("gla_ready"), 1)
            part(2)
            gelu_u(3)
            act.wait_ge(S("gmlp_ready"), 4)
            part(3)

            def begin(name, evict, n):
                split_hi(act, name, 0, 1)
                root(n)
                evict(0, 0)
                split_hi(act, name, 1, 0)
                evict(0, 1)

            paced(act, "out", split_hi, lambda i, j: None)
            for hf in range(HALVES):
                def gate(i, j):
                    if j == 0:
                        act.wait_ge(S("acc_read"), i * 2 + (tile0[f"up{hf}"] + 1))
                        nc.scalar.activation(tmp2, tmp1, ACT.Silu).then_inc(S("gate_ready"), 1)

                if hf == 0:
                    begin("up0", gate, 1)
                paced(act, f"up{hf}", split_hi, gate, start=1 if hf == 0 else 0)
                paced(act, f"down{hf}", split_hi, lambda i, j: None)
            act.wait_ge(S("p_loaded"), 16)
            nc.scalar.activation(p_hi, p_f[:, :, :], ACT.Copy).then_inc(S("p_hi_ready"), 1)

            def sigmoid(i, j):
                act.wait_ge(S("acc_read"), i * 2 + (tile0["ple"] + j + 1))
                nc.scalar.activation(tmp2, tmp1, ACT.Sigmoid).then_inc(S("ple_gate"), 1)

            begin("ple", sigmoid, 2)
            paced(act, "ple", split_hi, sigmoid, start=1)


        @block.vector
        def _(dve):
            link = Steps(dve, S("dve_step"))
            V = nc.vector

            for c in range(4):
                dve.wait_ge(S("x_hi_ready"), c + 1)
                for k in range(4 * c, 4 * c + 4):
                    ins = V.scalar_tensor_tensor(x_lo[:, k, :], x_f[:, k, :], gains[:, 0, k:k + 1],
                                                 x_hi[:, k, :].bitcast(F32), ALU.mult, ALU.subtract)
                ins.then_inc(S("x_ready"), 1)
                dve.wait_ge(S("w_hi_done") if c == 3 else S("w_quarter_hi"), 1 if c == 3 else c + 1)
                ws_ = slice(4 * c * P, 4 * (c + 1) * P)
                V.tensor_tensor(wlo[:, 0, ws_], raw[:, 0, ws_], whi[:, 0, ws_].bitcast(F32), ALU.subtract)\
                    .then_inc(S("w_lo_done") if c == 3 else S("w_quarter_lo"), 1)
            split_lo(dve, "in", 0, 1)
            dve.wait_ge(S("x_sq"), 2)
            V.tensor_reduce(ssq[:, :], proj[:, KT:KT + 8, :].rearrange("p k t -> p t k"), AX.X, ALU.add).then_inc(S("x_ssq"), 1)
            dve.wait_ge(S("x_ssq"), 1)
            dve.wait_ge(S("x_half"), 1)
            V.tensor_tensor(ssq[:, :], ssq[:, :], proj[:, KT + 8, :], ALU.add).then_inc(S("x_ssq"), 1)
            dve.wait_ge(S("small_loaded"), 32)
            link(V.tensor_scalar(small[:, 0:1], small[:, 0:1], HD ** -0.5, None, ALU.mult))

            def keep(t):
                dve.wait_ge(S("w_used"), t + 1)
                V.tensor_tensor(proj[:, ORDER[t], :], acc[:, t % 2, 0:T], rstd[:, :], ALU.mult).then_inc(S("acc_read"), 1)

            split_lo(dve, "in", 1, 0)
            dve.wait_ge(S("root_ready"), 1)
            keep(0)
            with dve.Fori(1, FIRST_ROWS // 2) as i:
                for j in range(2):
                    dve.wait_ge(S("w_used"), i * 2 + j)
                    V.tensor_tensor(proj[:, bass.ds(i * 2 + (j - 1 + ROW_QI), 1), :].rearrange("p o t -> p (o t)"),
                                    acc[:, 1 - j, 0:T], rstd[:, :], ALU.mult).then_inc(S("acc_read"), 1)
                    split_lo(dve, "in", i + j, 1 - j)
            keep(FIRST_ROWS - 1)

            def weights(_):
                dve.wait_ge(S("weights_mm"), 1)
                V.tensor_scalar(wi_n[:, :, :].rearrange("p a b -> p (a b)"), px[:, 3, 0:2 * IH],
                                ID ** -0.5 * IH ** -0.5, None, ALU.mult)
                V.tensor_tensor(wb[:, :, :], px[0:64, 3, 64:64 + TS].unsqueeze(1).broadcast_to([64, NB, TS]),
                                C["wbm"].rearrange("p (b t) -> p b t", b=NB), ALU.mult)
                V.tensor_copy(qi_s[:, :, :].rearrange("p b (j i) -> p b j i", i=NS),
                              proj[:, ROW_QI:ROW_QI + 8, SEQ:T].rearrange("p j (b i) -> p b j i", b=NB))
                V.tensor_copy(ki_s[:, :, PAST:T], proj[:, ROW_KI, SEQ:T].unsqueeze(1).broadcast_to([P, 2, TS]))\
                    .then_inc(S("weights_done"), 1)
                dve.wait_ge(S("weights_done"), 1)

            def bias_table(_):
                dve.wait_ge(S("btab_mm"), 1)
                V.tensor_copy(btab[:, :], px[0:NH, 2, 0:NDIST]).then_inc(S("btab_ready"), 1)

            def index(st):
                tt, q, nk = st // 4, st % 4, P * (st // 4 + 1)
                dve.wait_ge(S("relu_done"), st + 1)
                for e in range(2):
                    for jj in range(2):
                        head = 2 * (2 * q + jj) + e
                        src, w, dst = rl[:, 2 * e + jj, 0:nk], wi_n[:, tt, head:head + 1], sc[:, tt, 0:nk]
                        if q == 0 and e == 0 and jj == 0:
                            ins = V.tensor_scalar(dst, src, w, None, ALU.mult)
                        else:
                            ins = V.scalar_tensor_tensor(dst, src, w, dst, ALU.mult, ALU.add)
                        if (e, jj) != (1, 1):
                            link(ins)
                ins.then_inc(S("rl_free"), 1)
                dve.wait_ge(S("rl_free"), st + 1)

            def index_end(_):
                dve.wait_ge(S("idx_s_acc"), NB)
                V.tensor_copy(sc_s[:, 0:T], px[0:TS, 2, 0:T]).then_inc(S("sc_s_read"), 1)
                dve.wait_ge(S("sc_s_read"), 1)
                link(V.tensor_tensor(sc_s[:, PAST:T], sc_s[:, PAST:T], C["adm"], ALU.mult))
                link(V.tensor_tensor(sc_s[:, PAST:T], sc_s[:, PAST:T], C["admneg"], ALU.add))

            def rounds_of(work, best, rounds):
                for _ in range(rounds):
                    link(V.max(best, work))
                    link(V.match_replace(work, best, work, MARK))

            def pick(arg):
                tt, r0, r1 = arg
                nk = P * (tt + 1)
                if r0 == 0:
                    dve.wait_ge(S("scores_masked"), tt + 1)
                rounds_of(sc[:, tt, 0:nk], top8[:, :], r1 - r0)
                if r1 == KSEL_P // 8:
                    V.tensor_scalar(sc[:, tt, 0:nk], sc[:, tt, 0:nk], MARK, -1.0, ALU.not_equal, ALU.mult)\
                        .then_inc(S("picked"), 1)

            def pick_s(arg):
                r0, r1 = arg
                if r0 == 0:
                    dve.wait_ge(S("att_zero"), 1)
                rounds_of(sc_s[:, :], top8s[:, :], r1 - r0)
                if r1 == (KSEL_S + 7) // 8:
                    V.tensor_scalar(sc_s[:, 0:T], sc_s[:, 0:T], MARK, -1.0, ALU.not_equal, ALU.mult)\
                        .then_inc(S("sel_s_ready"), 1)

            def norm(n):
                row, g = NORMS[n]
                dve.wait_ge(S("norm_root"), n + 1)
                if n < 5:
                    pair = rows(row, row + 2)
                    ins = V.scalar_tensor_tensor(pair, pair, small[:, g:g + 1], sqb.rearrange("p a t -> p (a t)"),
                                                 ALU.mult, ALU.mult)
                else:
                    for r in range(2):
                        one_ = proj[:, row + r, :]
                        ins = V.scalar_tensor_tensor(one_, one_, small[:, g + r:g + r + 1], sqb[:, r, :],
                                                     ALU.mult, ALU.mult)
                ins.then_inc(S("norm_done"), 1)

            def softmax(u):
                nk = P * (u // 2 + 1)
                logits = px[:, 2:4, :].rearrange("p b s -> p (b s)")[:, 0:NR * nk].rearrange("p (r s) -> p r s", r=NR)
                dve.wait_ge(S("lg_ready"), u + 1)
                V.tensor_reduce(sm[:, 0:4], logits, AX.X, ALU.max, negate=True).then_inc(S("max_ready"), 1)
                dve.wait_ge(S("exp_ready"), u + 1)
                link(V.reciprocal(sm[:, 8:12], sm[:, 4:8]))
                pr = prob[:, 0:NR * nk].rearrange("p (r s) -> p r s", r=NR)
                V.tensor_tensor(pr, pr, sm[:, 8:12].unsqueeze(2).broadcast_to([P, NR, nk]), ALU.mult)\
                    .then_inc(S("p_ready"), 1)

            def gate(_):
                dve.wait_ge(S("gl_gate"), 1)
                for r in range(2):
                    ins = V.tensor_scalar(la[:, r, :], px[:, r, 0:T], small[:, 3 + r:4 + r], None, ALU.add)
                ins.then_inc(S("la_ready"), 1)

            kb, qb = proj[:, ROW_KB:ROW_KB + 2, :], proj[:, ROW_QB:ROW_QB + 2, :]
            def scan(_):
                V.tensor_scalar(qb, qb, BDK ** -0.5, None, ALU.mult).then_inc(S("qb_scaled"), 1)
                dve.wait_ge(S("lsp_ready"), 1)
                flat = [z.rearrange("p a t -> p (a t)") for z in (la, lsp)]
                link(V.scalar_tensor_tensor(flat[0], flat[0], 0.0, flat[1], ALU.min, ALU.subtract))
                for r in range(2):
                    ins = V.tensor_tensor_scan(bc[:, r, :], C["scan"], la[:, r, :], 0.0, ALU.mult, ALU.add)
                ins.then_inc(S("scanned"), 1)

            def level(m):
                dve.wait_ge(S("level_mm"), m + 1)
                if m == 0:
                    dve.wait_ge(S("att_zero"), 1)
                if m == 1:
                    V.tensor_copy(att_c[:, :, :, :], px[:, 0:2, 0:256].rearrange("p e (r t) -> p e r t", r=2))\
                        .then_inc(S("level_read"), 1)
                else:
                    mask = C["ident"] if m == 0 else C["lev"][:, (m - 2) * P:(m - 1) * P]
                    V.copy_predicated(att[:, :, :, :], mask.bitcast(U32).unsqueeze(1).unsqueeze(1).broadcast_to([P, 2, 4, P]),
                                      px[:, 0:2, :].rearrange("p e (a t) -> p e a t", a=4)).then_inc(S("level_read"), 1)
                    dve.wait_ge(S("level_read"), m + 1)
                if m < 8:
                    dve.wait_ge(S("e_level"), m + 1)
                    e1, e2, _, _ = blocks(dd[:, m % 2, :, :], m)
                    q2, k1 = blocks(qb, m)[1], blocks(kb, m)[0]
                    V.tensor_tensor(blocks(qe[:, m % 2], m)[1], q2, e2, ALU.mult)
                    V.tensor_tensor(blocks(ke[:, m % 2], m)[0], k1, e1, ALU.mult).then_inc(S("level_ready"), 1)

            def level_s(_):
                dve.wait_ge(S("level_s_mm"), 1)
                for n in range(3):
                    mask = [C["ident"], C["lev"][:, 5 * P:6 * P], C["lev"][:, 6 * P:7 * P]][n][0:TS, 0:TS].bitcast(U32)
                    ins = V.copy_predicated(att_s[:, :, :].rearrange("p e (r t) -> p e r t", r=2),
                                            mask.unsqueeze(1).unsqueeze(1).broadcast_to([TS, 2, 2, TS]),
                                            px[0:TS, 0:2, 2 * TS * n:2 * TS * (n + 1)].rearrange("p e (r t) -> p e r t", r=2))
                    if n < 2:
                        link(ins)
                ins.then_inc(S("level_s_read"), 1)

            def last(_):
                dve.wait_ge(S("level_ready"), 8)
                for r in range(2):
                    V.tensor_scalar(dd[:, 1, r, 0:SEQ], bc[:, r, 0:SEQ], bc[:, r, SEQ - 1:SEQ], None, ALU.subtract)
                bs = by_seq(bc[:, :, SEQ:T])
                V.tensor_tensor(by_seq(dd[:, 1, :, SEQ:T]), bs, bs[:, :, :, NS - 1:NS].broadcast_to([P, 2, NB, NS]),
                                ALU.subtract).then_inc(S("d_last"), 1)

            def decayed(_):
                dve.wait_ge(S("e_last"), 1)
                dve.wait_ge(S("norm_done"), 7)
                link(V.memset(qes[:, :, :, :, :], 0.0))
                for e in range(2):
                    pp = slice(64 * e, 64 * e + 64)
                    V.tensor_tensor(qes[pp, :, :, e, :], by_seq(proj[pp, ROW_QB:ROW_QB + 2, SEQ:T]), by_seq(ebs[pp, :, :]),
                                    ALU.mult)
                V.tensor_tensor(kdT, kb, dd[:, 1, :, :], ALU.mult).then_inc(S("kd_ready"), 1)

            def keys_s(_):
                link(V.memset(qpad[:, :, :, :], 0.0))
                for g in range(NG):
                    for b in range(NB):
                        V.tensor_copy(qpad[:, b, g, :].rearrange("p (t h) -> p t h", h=NH)[:, :, NR * g:NR * g + NR],
                                      proj[:, NR * g:NR * g + NR, SEQ + NS * b:SEQ + NS * b + NS].rearrange("p r t -> p t r"))
                dve.wait_ge(S("idx_mm"), 8)
                V.tensor_copy(k_s[:, :, :, PAST:T], proj[:, ROW_K:ROW_K + 2, SEQ:T].unsqueeze(1).broadcast_to([P, 4, 2, TS]))
                dve.wait_ge(S("bias_loaded"), 48)
                V.tensor_copy(bias_s[:, PAST:T].rearrange("p (b i) -> p b i", b=NB),
                              bias_n[:, :].unsqueeze(1).broadcast_to([TS, NB, NS])).then_inc(S("keys_s_ready"), 1)

            def softmax_s(x):
                dve.wait_ge(S("lg_s"), x + 1)
                V.tensor_reduce(sm[:, 16:17], px[:, x, 0:T], AX.X, ALU.max, negate=True).then_inc(S("max_s_ready"), 1)
                dve.wait_ge(S("exp_s_ready"), x + 1)
                link(V.reciprocal(sm[:, 18:19], sm[:, 17:18]))
                V.tensor_scalar(prob_s, prob_s, sm[:, 18:19], None, ALU.mult).then_inc(S("p_s_ready"), 1)

            def mix_s(x):
                dve.wait_ge(S("pv_s_mm"), x + 1)
                for g in range(NG):
                    ins = V.tensor_copy(proj[:, NR * g:NR * g + NR, SEQ + 16 * x:SEQ + 16 * x + 16],
                                        px[:, x, 64 * g:64 * g + 64].rearrange("p (t r) -> p r t", r=NR))
                ins.then_inc(S("mix_s_out"), 1)

            def outputs(_):
                ends = by_seq(ebs[:, :, :])[:, :, :, NS - 1].rearrange("p r b -> p b r")
                dve.wait_ge(S("o_mm"), 1)
                for half in range(2):
                    ins = V.tensor_tensor(s0[half], s0[half], ends[:, 4 * half:4 * half + 4, :].unsqueeze(3)
                                          .broadcast_to([P, 4, 2, BDV]), ALU.mult)
                ins.then_inc(S("s0_decayed"), 1)

            def out_norm(_):
                dve.wait_ge(S("o_root"), 1)
                link(V.scalar_tensor_tensor(ob.rearrange("p a t -> p (a t)"), ob.rearrange("p a t -> p (a t)"),
                                            small[:, 2:3], osq.rearrange("p a t -> p (a t)"), ALU.mult, ALU.mult))
                dve.wait_ge(S("silu_ready"), 1)
                V.tensor_tensor(proj[:, ROW_RB:ROW_RB + 4, :], ob, proj[:, ROW_RB:ROW_RB + 4, :], ALU.mult)\
                    .then_inc(S("gla_ready"), 1)

            def state_s(half):
                dve.wait_ge(S("ss_mm"), half + 1)
                dve.wait_ge(S("s0_decayed"), 1)
                bank = 0 if half else 4
                part = s0[half].rearrange("p b r v -> p (b r v)")
                V.tensor_tensor(part, part, px[:, bank:bank + 2, :].rearrange("p a b -> p (a b)"), ALU.add)\
                    .then_inc(S("state_s_ready"), 1)

            def spatial(_):
                dve.wait_ge(S("sp_gm"), 1)
                V.tensor_tensor(gsum[:, :, 0:SEQ].rearrange("p g (c t) -> p g c t", c=2),
                                px[:, 0:4, 0:SEQ].rearrange("p g (c t) -> p g c t", c=2),
                                bsp.unsqueeze(2).broadcast_to([P, 4, 2, P]), ALU.add)
                V.tensor_tensor(gsum[:, :, SEQ:T].rearrange("p g (b i) -> p g b i", b=NB),
                                px[:, 0:4, SEQ:T].rearrange("p g (b i) -> p g b i", b=NB),
                                bsp[:, :, 0:NS].unsqueeze(2).broadcast_to([P, 4, NB, NS]), ALU.add)\
                    .then_inc(S("gsum_ready"), 1)
                dve.wait_ge(S("gsum_ready"), 1)

            def gelu_u(r):
                dve.wait_ge(S("gelu_ready"), r + 1)
                V.tensor_tensor(proj[:, ROW_UC + r, :], gsum[:, r, :], proj[:, ROW_UC + r, :], ALU.mult)\
                    .then_inc(S("gmlp_ready"), 1)

            stages = dict(weights=weights, bias_table=bias_table, index=index, index_end=index_end, pick=pick, pick_s=pick_s, norm=norm,
                          softmax=softmax, gate=gate, scan=scan, level=level, level_s=level_s, last=last,
                          decayed=decayed, keys_s=keys_s, softmax_s=softmax_s, mix_s=mix_s, outputs=outputs,
                          gelu_u=gelu_u, out_norm=out_norm, spatial=spatial)
            for t in range(FIRST_ROWS, N_IN):
                if t + 1 < N_IN:
                    split_lo(dve, "in", (t + 1) // 2, (t + 1) % 2)
                else:
                    split_lo(dve, "out", 0, 0)
                keep(t)
                do(stages, t)
            for c in range(4):
                cs = slice(4 * c, 4 * c + 4)
                dve.wait_ge(S("m_hi_ready"), c + 1)
                V.tensor_tensor(m_lo[:, cs, :], proj[:, cs, :], m_hi[:, cs, :].bitcast(F32), ALU.subtract)\
                    .then_inc(S("m_ready"), 1)
                if c < 2:
                    state_s(c)
                if c == 2:
                    gelu_u(3)

            def one(ap, m):
                return ap[:, bass.ds(m, 1), :].rearrange("p o t -> p (o t)")

            def tile_into_h(m, bank, last_group, tile, gain, lk):
                dve.wait_ge(S("w_used"), last_group)
                hm = one(h, m)
                V.tensor_tensor(hm, hm, acc[:, bank, 0:T], ALU.add).then_inc(S("acc_read"), 1)
                if gain is None:
                    return
                dve.wait_ge(S("acc_read"), tile)
                lk(V.tensor_scalar(tmp1, hm, gains[:, gain, bass.ds(m, 1)], None, ALU.mult))
                lk(V.tensor_copy(one(n_hi, m), tmp1))
                V.tensor_tensor(one(n_lo, m), tmp1, one(n_hi, m).bitcast(F32), ALU.subtract)\
                    .then_inc(S("n_ready"), 1)

            def rounds(name, evict_pair, per):
                base, n, *_ = stream[name]
                if n > 2:
                    with dve.Fori(0, n // 2 - 1) as i, link.each(i, n // 2 - 1, per) as lk:
                        split_lo(dve, name, i, 1)
                        evict_pair(i, 0, lk)
                        split_lo(dve, name, i + 1, 0)
                        evict_pair(i, 1, lk)
                i = n // 2 - 1
                split_lo(dve, name, i, 1)
                evict_pair(i, 0, link)
                if name in following:
                    split_lo(dve, following[name], 0, 0)
                evict_pair(i, 1, link)

            b0, t0 = stream["out"][0], tile0["out"]

            def into_h(i, j, lk):
                dve.wait_ge(S("h_loaded"), 32)
                dve.wait_ge(S("state_stored"), 16 * 3)
                tile_into_h(i * 2 + j, j, i * 2 + (b0 + j + 1), i * 2 + (t0 + j + 1), 1, lk)

            rounds("out", into_h, 4)
            for hf in range(HALVES):
                ub, ut = stream[f"up{hf}"][0], tile0[f"up{hf}"]

                def hidden(i, j, lk):
                    dve.wait_ge(S("w_used"), i * 2 + (ub + j + 1))
                    dve.wait_ge(S("root_ready"), 2)
                    if j == 0:
                        V.tensor_tensor(tmp1, acc[:, 0, 0:T], rstd[:, :], ALU.mult).then_inc(S("acc_read"), 1)
                        return
                    V.tensor_tensor(tmp3, acc[:, 1, 0:T], rstd[:, :], ALU.mult).then_inc(S("acc_read"), 1)
                    dve.wait_ge(S("acc_read"), i * 2 + (ut + 2))
                    dve.wait_ge(S("gate_ready"), i + (hf * FH + 1))
                    lk(V.tensor_tensor(tmp3, tmp3, tmp2, ALU.mult))
                    lk(V.tensor_copy(one(a_hi, i), tmp3))
                    V.tensor_tensor(one(a_lo, i), tmp3, one(a_hi, i).bitcast(F32), ALU.subtract)\
                        .then_inc(S("a_ready"), 1)
                    dve.wait_ge(S("a_ready"), i + (hf * FH + 1))

                rounds(f"up{hf}", hidden, 2)
                db, dt = stream[f"down{hf}"][0], tile0[f"down{hf}"]
                gain = 2 if hf == HALVES - 1 else None
                name = f"down{hf}"
                per = 0 if gain is None else 4
                with dve.Fori(0, N_OUT // 2 - 1) as i, link.each(i, N_OUT // 2 - 1, per) as lk:
                    split_lo(dve, name, i * 2, 1)
                    split_lo(dve, name, i * 2 + 1, 0)
                    tile_into_h(i * 2, 0, i * 4 + (db + 2), i * 2 + (dt + 1), gain, lk)
                    split_lo(dve, name, i * 2 + 1, 1)
                    split_lo(dve, name, i * 2 + 2, 0)
                    tile_into_h(i * 2 + 1, 1, i * 4 + (db + 4), i * 2 + (dt + 2), gain, lk)
                i = N_OUT // 2 - 1
                split_lo(dve, name, i * 2, 1)
                split_lo(dve, name, i * 2 + 1, 0)
                tile_into_h(i * 2, 0, i * 4 + (db + 2), i * 2 + (dt + 1), gain, link)
                split_lo(dve, name, i * 2 + 1, 1)
                split_lo(dve, following[name], 0, 0)
                tile_into_h(i * 2 + 1, 1, i * 4 + (db + 4), i * 2 + (dt + 2), gain, link)
            dve.wait_ge(S("p_hi_ready"), 1)
            V.tensor_tensor(p_lo, p_f[:, :, :], p_hi.bitcast(F32), ALU.subtract).then_inc(S("p_ready2"), 1)
            pb, pt0 = stream["ple"][0], tile0["ple"]

            def ple(i, j, lk):
                dve.wait_ge(S("w_used"), i * 2 + (pb + j + 1))
                dve.wait_ge(S("root_ready"), 3)
                V.tensor_tensor(tmp1, acc[:, j, 0:T], rstd[:, :], ALU.mult).then_inc(S("acc_read"), 1)
                dve.wait_ge(S("ple_gate"), i * 2 + (j + 1))
                lk(V.tensor_tensor(tmp3, tmp2, px[:, j, 0:T], ALU.mult))
                hm = one(h, i * 2 + j)
                V.tensor_tensor(hm, hm, tmp3, ALU.add).then_inc(S("y_ready"), 1)
                dve.wait_ge(S("y_ready"), i * 2 + (j + 1))

            rounds("ple", ple, 2)


        @block.tensor
        def _(pe):
            M = nc.tensor.matmul
            tr = nc.tensor.transpose
            ident = C["ident"]

            def group(name, i, j, out, k0, kt, hi_, lo_, **kw):
                base = stream[name][0]
                pe.wait_ge(S("w_lo_done"), i * 2 + (base + j + 1))
                products(out, j, k0, kt, hi_, lo_, **kw).then_inc(S("w_used"), 1)

            def tile_free(name, i, per, j):
                if isinstance(i, int) and tile0[name] + per * i + j < 2:
                    return
                pe.wait_ge(S("acc_read"), i * per + (tile0[name] + j - 1))

            def mean_squares(n):
                M(px[:, 5, 0:T], ones[:, :], ssq[:, :], start=True, stop=True).then_inc(S("ms_mm"), 1)

            for c in range(4):
                pe.wait_ge(S("x_ready"), c + 1)
                pe.wait_ge(S("w_lo_done") if c == 3 else S("w_quarter_lo"), 1 if c == 3 else c + 1)
                ins = products(acc[:, 0, 0:T], 0, 4 * c, 4, x_hi, x_lo, first=c == 0, last=c == 3, at=4 * c)
            ins.then_inc(S("w_used"), 1)
            pe.wait_ge(S("w_lo_done"), 2)
            products(acc[:, 1, 0:T], 1, 0, KT // 2, x_hi, x_lo, last=False)
            pe.wait_ge(S("x_ssq"), 2)
            pe.wait_ge(S("ones_ready"), 1)
            mean_squares(0)
            products(acc[:, 1, 0:T], 1, KT // 2, KT // 2, x_hi, x_lo, first=False, at=KT // 2).then_inc(S("w_used"), 1)
            with pe.Fori(1, FIRST_ROWS // 2) as i:
                for j in range(2):
                    tile_free("in", i, 2, j)
                    group("in", i, j, acc[:, j, 0:T], 0, KT, x_hi, x_lo)

            def weights(_):
                pe.wait_ge(S("acc_read"), kept(ROW_MISC))
                pe.wait_ge(S("consts_loaded"), 32)
                for tt in range(2):
                    tr(px[:, 3, IH * tt:IH * tt + IH], proj[0:IH, ROW_MISC, P * tt:P * tt + P], ident[0:IH, 0:IH])
                M(px[0:64, 3, 64:64 + TS], C["e16"], proj[0:IH, ROW_MISC, SEQ:T], start=True, stop=True)\
                    .then_inc(S("weights_mm"), 1)

            def bias_table(_):
                M(px[0:NH, 2, 0:NDIST], relb[:, :], C["bucket"], start=True, stop=True).then_inc(S("btab_mm"), 1)

            def index(st):
                tt, q, nk = st // 4, st % 4, P * (st // 4 + 1)
                if st:
                    pe.wait_ge(S("relu_done"), st)
                for jj in range(2):
                    for e in range(2):
                        pp = slice(64 * e, 64 * e + 64)
                        ins = M(px[:, e, 256 * jj:256 * jj + nk],
                                proj[pp, ROW_QI + 2 * q + jj, P * tt:P * tt + P], proj[pp, ROW_KI, 0:nk],
                                start=True, stop=True)
                ins.then_inc(S("idx_mm"), 1)

            def index_sum(b):
                pe.wait_ge(S("relu_s_done"), 2 * b + 2)
                pe.wait_ge(S("btab_ready"), 1)
                M(px[0:TS, 2, 0:T], wb[:, b, :], rl_s[:, b % 2, :], start=b == 0, stop=b == NB - 1)\
                    .then_inc(S("idx_s_acc"), 1)

            def index_s(b):
                pe.wait_ge(S("weights_done"), 1)
                pe.wait_ge(S("root_ready"), 1)
                pe.wait_ge(S(f"ki_page{b % 2}"), 32 * (b // 2 + 1))
                if b:
                    pe.wait_ge(S("relu_s_done"), 2 * b)
                for e in range(2):
                    ins = M(px[32 * e:32 * e + 32, 4 + e, 0:T], qi_s[64 * e:64 * e + 64, b, :],
                            ki_s[64 * e:64 * e + 64, b % 2, :], start=True, stop=True)
                ins.then_inc(S("idx_s_mm"), 1)
                if b:
                    index_sum(b - 1)

            def norm(n):
                bank = 0 if n < 5 else 2
                if n in (0, 5):
                    pe.wait_ge(S("mix_out") if n else S("relu_done"), 4 if n else 8)
                else:
                    pe.wait_ge(S("norm_root"), n)
                pe.wait_ge(S("norm_sq"), n + 1)
                for r in range(2):
                    ins = M(px[:, bank + r, 0:T], ones[:, :], sqb[:, r, :], start=True, stop=True)
                ins.then_inc(S("norm_mm"), 1)

            def values(_):
                pe.wait_ge(S("relu_s_done"), 2 * NB)
                pe.wait_ge(S("acc_read"), kept(ROW_V + 1))
                for tt, w in enumerate(widths):
                    for g in range(NG):
                        col = 256 * (tt % 2) + g * HD
                        ins = tr(px[0:w, 4 + tt // 2, col:col + HD], proj[:, ROW_V + g, P * tt:P * tt + w], ident)
                ins.then_inc(S("values_mm"), 1)

            def softmax(u):
                tt, g, nk = u // 2, u % 2, P * (u // 2 + 1)
                per = 512 // nk
                if u == 0:
                    pe.wait_ge(S("sc_s_read"), 1)
                    pe.wait_ge(S("bias_loaded"), 48)
                else:
                    pe.wait_ge(S("mix_out"), u)
                pe.wait_ge(S("sel_ready"), tt + 1)
                pe.wait_ge(S("norm_done"), 5)
                for r0 in range(0, NR, per):
                    bank = px[:, 2 + r0 * nk // 512, :]
                    M(bank, ident, bias_p[:, NR * g + r0:NR * g + r0 + per, SEQ - nk:SEQ], start=True, stop=False)
                    M(bank, C["bigI"], sc[:, tt, 0:nk].unsqueeze(1).broadcast_to([P, per, nk]), start=False, stop=False)
                    for r in range(per):
                        ins = M(bank[:, r * nk:(r + 1) * nk], proj[:, NR * g + r0 + r, P * tt:P * tt + P],
                                proj[:, ROW_K + g, 0:nk], start=False, stop=r == per - 1)
                ins.then_inc(S("lg_ready"), 1)

            def transpose(u):
                tt, nk = u // 2, P * (u // 2 + 1)
                pe.wait_ge(S("p_ready"), u + 1)
                pe.wait_ge(S("pt_ready") if u else S("vnat_ready"), max(u, 1))
                if u == 2:
                    pe.wait_ge(S("pt_s_ready"), 2)
                for s in range(tt + 1):
                    for r in range(NR):
                        ins = tr(px[:, 4 + s, P * r:P * r + P], prob[:, r * nk + P * s:r * nk + P * s + P], ident)
                ins.then_inc(S("pt_mm"), 1)

            def mix(u):
                tt, g = u // 2, u % 2
                pe.wait_ge(S("pt_ready"), u + 1)
                for s in range(tt + 1):
                    ins = M(px[:, 2, :], vnat[:, s, g * HD:(g + 1) * HD], pt[:, NR * P * s:NR * P * (s + 1)],
                            start=s == 0, stop=s == tt)
                ins.then_inc(S("mix_mm"), 1)

            def gate(_):
                pe.wait_ge(S("wgb_loaded"), 16)
                pe.wait_ge(S("norm_root"), 5)
                for r in range(2):
                    ins = M(px[:, r, 0:T], wgb[GB0:GB0 + RANK, r * P:(r + 1) * P], proj[GB0:GB0 + RANK, ROW_MISC, :],
                            start=True, stop=True)
                ins.then_inc(S("gl_gate"), 1)

            def pairs(m):
                if m == 0:
                    return proj[:, ROW_QB:ROW_QB + 2, :], proj[:, ROW_KB:ROW_KB + 2, :]
                return qe[:, (m - 1) % 2], ke[:, (m - 1) % 2]

            def level(m):
                q_, k_ = pairs(m)
                if m:
                    pe.wait_ge(S("level_ready"), m)
                    pe.wait_ge(S("level_read"), m)
                else:
                    pe.wait_ge(S("mix_s_out"), 2)
                    pe.wait_ge(S("qb_scaled"), 1)
                for tt in range(1 if m == 1 else 2):
                    tq = 1 if m == 1 else tt
                    for r in range(2):
                        for e in range(2):
                            pp = slice(64 * e, 64 * e + 64)
                            ins = M(px[:, e, 256 * tt + P * r:256 * tt + P * r + P], k_[pp, r, P * tt:P * tt + P],
                                    q_[pp, r, P * tq:P * tq + P], start=True, stop=True)
                ins.then_inc(S("level_mm"), 1)

            def level_s(_):
                pe.wait_ge(S("level_read"), 9)
                for n, m in enumerate((0, 7, 8)):
                    q_, k_ = pairs(m)
                    for r in range(2):
                        for e in range(2):
                            pp = slice(64 * e, 64 * e + 64)
                            ins = M(px[0:TS, e, TS * (2 * n + r):TS * (2 * n + r) + TS], k_[pp, r, SEQ:T], q_[pp, r, SEQ:T],
                                    start=True, stop=True)
                ins.then_inc(S("level_s_mm"), 1)

            def vn_nat(_):
                pe.wait_ge(S("norm_done"), 7)
                for tt, w in enumerate(widths):
                    for g in range(4):
                        ins = tr(px[0:w, [4, 5, 3][tt], P * g:P * g + P], proj[:, ROW_VC + g, P * tt:P * tt + w], ident)
                ins.then_inc(S("vn_mm"), 1)

            def vb_nat(_):
                pe.wait_ge(S("vnn_ready"), 1)
                for tt, w in enumerate(widths):
                    for q in range(BH):
                        ins = tr(px[0:w, [2, 3, 4][tt], P * q:P * q + P], proj[:, ROW_VB + q, P * tt:P * tt + w], ident)
                ins.then_inc(S("vb_mm"), 1)

            def softmax_s(x):
                pe.wait_ge(S("la_ready"), 1)
                pe.wait_ge(S("sel_s_ready"), 1)
                pe.wait_ge(S("keys_s_ready"), 1)
                out = px[:, x, 0:T]
                M(out, C["ex"][:, P * x:P * x + P], sc_s[:, 0:T], start=True, stop=False)
                M(out, C["eb"], bias_s[:, :], start=False, stop=False)
                for b4 in range(4):
                    pe.wait_ge(S(f"k_page{b4}"), 32 * (x + 1))
                    for g in range(NG):
                        ins = M(out[32 * b4:32 * b4 + 32, :], qpad[:, 4 * x + b4, g, :], k_s[:, b4, g, :],
                                start=False, stop=g == NG - 1)
                ins.then_inc(S("lg_s"), 1)

            def transpose_s(x):
                pe.wait_ge(S("p_s_ready"), x + 1)
                pe.wait_ge(S("pt_s_ready") if x else S("vnat_ready"), 1)
                for s, w in enumerate(widths):
                    ins = tr(px[0:w, 5, P * s:P * s + P], prob_s[:, P * s:P * s + w], ident)
                ins.then_inc(S("pt_s_mm"), 1)

            def mix_s(x):
                pe.wait_ge(S("pt_s_ready"), x + 1)
                pr = [pt_s[0:w, P * s:P * s + P].rearrange("p (b t h) -> p b t h", b=4, h=NH) for s, w in enumerate(widths)]
                for g in range(NG):
                    M(px[:, x, 64 * g:64 * g + 64], vnat[0:TS, 2, g * HD:(g + 1) * HD], pr[2][:, :, :, NR * g:NR * g + NR],
                      start=g == 0, stop=False)
                for b4 in range(4):
                    pe.wait_ge(S(f"v_page{b4}"), 32 * (x + 1))
                    for g in range(NG):
                        col = 64 * g + 16 * b4
                        for s in range(NPG):
                            ins = M(px[:, x, col:col + 16], v_s[:, b4, s, g * HD:(g + 1) * HD],
                                    pr[s][:, b4, :, NR * g:NR * g + NR], start=False,
                                    stop=(b4, g, s) == (3, NG - 1, NPG - 1))
                ins.then_inc(S("pv_s_mm"), 1)

            def kd_nat(_):
                pe.wait_ge(S("kd_ready"), 1)
                pe.wait_ge(S("vnn_ready"), 1)
                pe.wait_ge(S("level_s_read"), 1)
                for tt, w in enumerate(widths):
                    for r in range(2):
                        dst = px[0:w, 5, 256 * tt + P * r:256 * tt + P * r + P] if tt < 2 else px[0:w, 0, P * r:P * r + P]
                        ins = tr(dst, kdT[:, r, P * tt:P * tt + w], ident)
                ins.then_inc(S("kd_mm"), 1)

            def outputs(_):
                pe.wait_ge(S("gsum_ready"), 1)
                pe.wait_ge(S("s0_loaded"), 32)
                for r in range(2):
                    for e in range(2):
                        hd = 2 * r + e
                        vs = slice(BDV * hd, BDV * hd + BDV)
                        M(px[:, hd, 0:P], vbn[:, 0, vs], att[:, e, r, :], start=True, stop=True)
                        M(px[:, hd, P:SEQ], vbn[:, 0, vs], att_c[:, e, r, :], start=True, stop=False)
                        M(px[:, hd, P:SEQ], vbn[:, 1, vs], att[:, e, 2 + r, :], start=False, stop=True)
                        M(out_s(r)[:, :, e, :], vbn[0:TS, 2, vs],
                          att_s[:, e, TS * r:TS * r + TS].rearrange("p (b i) -> p b i", b=NB), start=hd == 0, stop=False)
                    for b in range(NB):
                        ins = M(out_s(r)[:, b, :, :], s0[b // 4][:, b % 4, r, :], qes[:, r, b, :, :], start=False,
                                stop=(r, b) == (1, NB - 1))
                ins.then_inc(S("o_mm"), 1)

            def state_p(_):
                pe.wait_ge(S("kdn_ready"), 1)
                for r in range(2):
                    for e in range(2):
                        hd = 2 * r + e
                        for tt in range(2):
                            ins = M(px[64 * e:64 * e + 64, 5, P * r:P * r + P], kdn[:, tt, 64 * hd:64 * hd + 64],
                                    vbn[:, tt, BDV * hd:BDV * hd + BDV], start=tt == 0, stop=tt == 1)
                ins.then_inc(S("sp_mm"), 1)

            def out_norm(_):
                pe.wait_ge(S("osq_ready"), 1)
                for q in range(BH):
                    ins = M(px[:, q, 0:T], ones[:, :], osq[:, q, :], start=True, stop=True)
                ins.then_inc(S("o_ssq"), 1)

            def state_s(half):
                pe.wait_ge(S("kdm_ready"), 1)
                pe.wait_ge(S("o_root") if half else S("state_p_ready"), 1)
                bank = 0 if half else 4
                for b in range(4):
                    for r in range(2):
                        for e in range(2):
                            hd, place = 2 * r + e, 2 * b + r
                            ins = M(px[64 * e:64 * e + 64, bank + place // 4, P * (place % 4):P * (place % 4) + P],
                                    kdm[:, 4 * half + b, 64 * hd:64 * hd + 64], vbn[0:TS, 2, BDV * hd:BDV * hd + BDV],
                                    start=True, stop=True)
                ins.then_inc(S("ss_mm"), 1)

            def spatial(_):
                pe.wait_ge(S("kdn_ready"), 1)
                pe.wait_ge(S("vbn_ready"), 1)
                pe.wait_ge(S("ws_ready"), 1)
                for g in range(4):
                    cs = slice(P * g, P * g + P)
                    for tt in range(2):
                        M(px[:, g, P * tt:P * tt + P], vnn[:, tt, cs], ws[:, g, :], start=True, stop=True)
                    ins = M(px[:, g, SEQ:T], vnn[0:TS, 2, cs], wss[:, g, :], start=True, stop=True)
                ins.then_inc(S("sp_gm"), 1)

            stages = dict(weights=weights, bias_table=bias_table, index=index, index_s=index_s, index_end=lambda _: index_sum(NB - 1),
                          norm=norm, values=values, softmax=softmax, transpose=transpose, mix=mix, gate=gate,
                          level=level, level_s=level_s, vn_nat=vn_nat, vb_nat=vb_nat, softmax_s=softmax_s,
                          transpose_s=transpose_s, mix_s=mix_s, kd_nat=kd_nat, outputs=outputs, state_p=state_p,
                          out_norm=out_norm, state_s=state_s, spatial=spatial)
            for t in range(FIRST_ROWS, N_IN):
                tile_free("in", t // 2, 2, t % 2)
                group("in", t // 2, t % 2, acc[:, t % 2, 0:T], 0, KT, x_hi, x_lo)
                do(stages, t)
            state_s(1)

            tile_free("out", 0, 2, 0)
            pe.wait_ge(S("w_lo_done"), N_IN + 1)
            for c in range(4):
                pe.wait_ge(S("m_ready"), c + 1)
                ins = products(acc[:, 0, 0:T], 0, 4 * c, 4, m_hi, m_lo, first=c == 0, last=c == 3, at=4 * c)
            ins.then_inc(S("w_used"), 1)
            tile_free("out", 0, 2, 1)
            group("out", 0, 1, acc[:, 1, 0:T], 0, KT, m_hi, m_lo)
            with pe.Fori(1, N_OUT // 2) as i:
                for j in range(2):
                    tile_free("out", i, 2, j)
                    group("out", i, j, acc[:, j, 0:T], 0, KT, m_hi, m_lo)
            def behind_norm(name, n, hi_, lo_):
                tile_free(name, 0, 2, 0)
                pe.wait_ge(S("w_lo_done"), stream[name][0] + 1)
                pe.wait_ge(S("n_ready"), n * KT - 1)
                products(acc[:, 0, 0:T], 0, 0, KT - 1, hi_, lo_, last=False)
                pe.wait_ge(S("n_ready"), n * KT)
                ins = products(acc[:, 0, 0:T], 0, KT - 1, 1, hi_, lo_, first=False, at=KT - 1)
                if name != "ple":
                    ins.then_inc(S("w_used"), 1)
                pe.wait_ge(S("ssq_added"), n * KT)
                mean_squares(n)

            for hf in range(HALVES):
                if hf == 0:
                    behind_norm("up0", 1, n_hi, n_lo)
                    tile_free("up0", 0, 2, 1)
                    group("up0", 0, 1, acc[:, 1, 0:T], 0, KT, n_hi, n_lo)
                with pe.Fori(1 if hf == 0 else 0, FH) as i:
                    for j in range(2):
                        tile_free(f"up{hf}", i, 2, j)
                        group(f"up{hf}", i, j, acc[:, j, 0:T], 0, KT, n_hi, n_lo)
                def down(i, j):
                    tile_free(f"down{hf}", i, 2, j)
                    for kk in range(2):
                        if isinstance(i, int) and kk == 1:
                            pe.wait_ge(S("a_ready"), FH * (hf + 1))
                        group(f"down{hf}", i * 2 + j, kk, acc[:, j, 0:T], kk * DK, DK, a_hi, a_lo,
                              first=kk == 0, last=kk == 1)

                pe.wait_ge(S("a_ready"), FH * hf + DK)
                for j in range(2):
                    down(0, j)
                with pe.Fori(1, N_OUT // 2) as i:
                    for j in range(2):
                        down(i, j)
            def ple(i, j):
                base = stream["ple"][0]
                tile_free("ple", i, 2, j)
                pe.wait_ge(S("w_lo_done"), i * 2 + (base + j + 1))
                products(acc[:, j, 0:T], j, 0, KT, n_hi, n_lo)
                if not isinstance(i, int):
                    pe.wait_ge(S("y_ready"), i * 2 + (j - 1))
                inputs(j)

            def inputs(j):
                products(px[:, j, 0:T], j, 0, GK - KT, p_hi, p_lo, at=KT).then_inc(S("w_used"), 1)

            behind_norm("ple", 2, n_hi, n_lo)
            pe.wait_ge(S("p_ready2"), 1)
            inputs(0)
            ple(0, 1)
            with pe.Fori(1, N_OUT // 2) as i:
                for j in range(2):
                    ple(i, j)


SHAPES = {"yT": (P, KT, T), "kvT": (P, 4, T), "kiT": (ID, T), "gla_p": (P, 2, BDV), "gla_s": (P, NB, 2, BDV),
          "vn_s": (P, 4, TS)}


def tiles(w, kt):
    k, m = w.shape
    return np.ascontiguousarray(w.reshape(kt, P, m // P, P).transpose(2, 1, 0, 3).reshape(m // P, P, kt * P))


def kernel(**inputs):
    import concourse.bacc as bacc
    from concourse.bass_utils import run_bass_kernel_spmd

    x = {k: np.asarray(v) for k, v in inputs.items()}

    def featT(p, s, n):
        both = np.concatenate([p.reshape(SEQ, n * P), s.reshape(TS, n * P)])
        return np.ascontiguousarray(both.T.reshape(n, P, T).transpose(1, 0, 2))

    w = x["w_in"][0]
    edges = np.cumsum([0, NH * HD, NG * HD, NG * HD, IH * ID, ID, IH, BH * BDK, BH * BDK, BH * BDV, RANK,
                       BH * BDV, 4 * P, 4 * P])
    q, k, v, qi, ki, wi, qb, kb, vb, gb, rb, uc, vc = [w[:, s:e] for s, e in zip(edges, edges[1:])]
    misc = np.zeros((D, P), w.dtype)
    misc[:, 0:IH] = wi
    misc[:, GB0:GB0 + RANK] = gb
    w_in = np.concatenate([qi, ki, ki, misc, q, k, v, qb, kb, vb, vc, rb, uc], axis=1)
    gate, up = tiles(x["w_ffn_gate"][0], KT), tiles(x["w_ffn_up"][0], KT)
    down = x["w_ffn_down"][0].reshape(HALVES, 2, DK, P, N_OUT, P).transpose(0, 4, 1, 3, 2, 5)
    small = np.concatenate([x["q_norm_g"][0][:, None], x["k_norm_g"][0][:, None], x["g_out_b"][0][:, None],
                            x["b_gate_b"][0].reshape(2, P).T, x["g_v_c"][0].reshape(4, P).T], axis=1)
    w_sp = x["w_spatial"][0].transpose(2, 0, 1)
    arrays = {
        "xT": featT(x["x_prompt"], x["x_sample"], KT),
        "pT": featT(x["p_prompt"], x["p_sample"], PLE // P),
        "gains": np.stack([x[g][0].reshape(KT, P).T for g in ("g_mix", "g_ffn", "g_ple")], axis=1),
        "small": small,
        "pages": x["page_table"].reshape(1, NB * NPG).astype(np.int32),
        "w_in": tiles(w_in, KT),
        "w_out": tiles(x["w_out"][0], KT),
        "w_gu": np.stack([gate, up], axis=1).reshape(2 * FT, P, KT * P),
        "w_down": down.reshape(HALVES * N_OUT * 2, P, DK * P),
        "w_ple": np.concatenate([tiles(x["w_ple_gate"][0], KT), tiles(x["w_ple_proj"][0], PLE // P)], axis=2),
        "cache_k": x["cache_k"][0].transpose(0, 3, 2, 1),
        "cache_v": x["cache_v"][0].reshape(NPOOL, PAGE, NG * HD),
        "cache_ik": np.tile(x["cache_idx_k"][0].transpose(0, 2, 1), (1, 2, 1)),
        "state": x["state_gla"][0].reshape(NB, 2, 2, BDK, BDV).transpose(2, 3, 0, 1, 4).reshape(P, NB, 2, BDV),
        "rel_bias": x["rel_bias"],
        "w_gate_b": x["w_gate_b"][0],
        "w_sp": w_sp,
        "w_sps": np.tile(w_sp[0:NS, :, 0:NS], (NB, 1, NB)),
        "b_sp": x["b_spatial"][0].reshape(4 * P),
        "consts": constants(),
    }
    arrays = {k_: np.ascontiguousarray(v_) for k_, v_ in arrays.items()}
    nc = bacc.Bacc("TRN2", target_bir_lowering=False, num_devices=1)
    a = {n: nc.dram_tensor(f"in_{n}", z.shape, mybir.dt.from_np(z.dtype), kind="ExternalInput").ap()
         for n, z in arrays.items()}
    o = {n: nc.dram_tensor(f"out_{n}", s, F32, kind="ExternalOutput").ap() for n, s in SHAPES.items()}
    build_layer(nc, a, o)
    r = run_bass_kernel_spmd(nc, [{f"in_{n}": z for n, z in arrays.items()}], core_ids=[0])
    y, kv, kiT, gp, gs, vn = [np.asarray(r.results[0][f"out_{n}"]) for n in SHAPES]
    y = y.transpose(2, 1, 0).reshape(T, D)
    kv = kv.transpose(2, 1, 0)
    kk, vv, ki_ = kv[:, 0:2], kv[:, 2:4], kiT.T

    def states(z, n):
        return z.reshape(2, BDK, n, 2, BDV).transpose(2, 3, 0, 1, 4).reshape(1, n, BH, BDK, BDV)

    return (y[:SEQ].reshape(1, SEQ, D), y[SEQ:].reshape(NB, NS, D),
            kk[:SEQ].reshape(1, 1, SEQ, NG, HD), vv[:SEQ].reshape(1, 1, SEQ, NG, HD),
            ki_[:SEQ].reshape(1, 1, SEQ, ID), states(gp, 1),
            kk[SEQ:].reshape(1, NB, NS, NG, HD), vv[SEQ:].reshape(1, NB, NS, NG, HD),
            ki_[SEQ:].reshape(1, NB, NS, ID), states(gs, NB),
            vn.transpose(2, 1, 0).reshape(1, NB, NS, 4 * P))
```
